# Optimizing a Trainium2 kernel written in Bass

```python
import math
import jax, jax.numpy as jnp
from jax import lax
import numpy as np

D_MODEL = 1024
BATCH = 1
SEQ = 256
DEPTH = 1

ATTN_HEADS = 8
HEAD_DIM = 64
ATTN_W = ATTN_HEADS * HEAD_DIM
MOBA_BLOCK = 256
MOBA_TOPK = 3
Q_CHUNK = 64
POOL_GROUPS = 4
POOL_GROUP_W = 128
POOL_W = POOL_GROUPS * POOL_GROUP_W
POOL_WINDOWS = (2, 4, 8, 16)
NUM_BUCKETS = 32
MAX_DISTANCE = 128
D_FF = 2816
CONV_W = 3
EPS = 1e-6
IN_W = 3 * ATTN_W + POOL_W + 2 * D_MODEL


def rms_norm(x, gain):
    xf = x.astype(jnp.float32)
    y = xf * lax.rsqrt(jnp.mean(xf * xf, axis=-1, keepdims=True) + EPS)
    return (y * gain.astype(jnp.float32)).astype(x.dtype)

def t5_bucket(dist):
    max_exact = NUM_BUCKETS // 2
    n = jnp.maximum(dist, 0)
    nf = jnp.maximum(n, 1).astype(jnp.float32)
    large = max_exact + (jnp.log(nf / max_exact) / math.log(MAX_DISTANCE / max_exact)
                         * (NUM_BUCKETS - max_exact)).astype(jnp.int32)
    large = jnp.minimum(large, NUM_BUCKETS - 1)
    return jnp.where(n < max_exact, n, large)

def moba_attention(q, k, v, rel_bias):
    B, H, S, Dh = q.shape
    n_blocks = -(-S // MOBA_BLOCK)
    s_pad = n_blocks * MOBA_BLOCK
    pad = ((0, 0), (0, 0), (0, s_pad - S), (0, 0))
    q = jnp.pad(q, pad)
    k = jnp.pad(k, pad)
    v = jnp.pad(v, pad)
    k_blocks = k.reshape(B, H, n_blocks, MOBA_BLOCK, Dh)
    v_blocks = v.reshape(B, H, n_blocks, MOBA_BLOCK, Dh)
    k_mean = jnp.mean(k_blocks.astype(jnp.float32), axis=3).astype(k.dtype)

    pos = jnp.arange(s_pad)
    q_blk = pos // MOBA_BLOCK
    gate = jnp.einsum('bhsd,bhnd->bhsn', q, k_mean).astype(jnp.float32)
    past = jnp.arange(n_blocks)[None, :] < q_blk[:, None]
    gate = jnp.where(past[None, None], gate, -jnp.inf)
    k_sel = min(MOBA_TOPK, n_blocks)
    _, sel = lax.top_k(gate, k_sel)
    sel_valid = jnp.arange(k_sel)[None, :] < q_blk[:, None]

    n_chunks = s_pad // Q_CHUNK
    q_c = q.reshape(B, H, n_chunks, Q_CHUNK, Dh).transpose(2, 0, 1, 3, 4)
    sel_c = sel.reshape(B, H, n_chunks, Q_CHUNK, k_sel).transpose(2, 0, 1, 3, 4)
    valid_c = sel_valid.reshape(n_chunks, Q_CHUNK, k_sel)
    bias_t = rel_bias.T.astype(jnp.float32)
    b_idx = jnp.arange(B)[:, None, None, None]
    h_idx = jnp.arange(H)[None, :, None, None]
    offs = jnp.arange(MOBA_BLOCK)
    scale = HEAD_DIM ** -0.5
    n_sel = k_sel * MOBA_BLOCK

    def chunk_fn(args):
        ci, qc, selc, validc = args
        qpos = ci * Q_CHUNK + jnp.arange(Q_CHUNK)
        own = (ci * Q_CHUNK) // MOBA_BLOCK
        k_own = lax.dynamic_index_in_dim(k_blocks, own, axis=2, keepdims=False)
        v_own = lax.dynamic_index_in_dim(v_blocks, own, axis=2, keepdims=False)
        dist_own = qpos[:, None] - (own * MOBA_BLOCK + offs)[None, :]
        bias_own = bias_t[:, t5_bucket(dist_own)]
        logit_own = jnp.einsum('bhqd,bhkd->bhqk', qc, k_own).astype(jnp.float32) * scale + bias_own
        logit_own = jnp.where(dist_own >= 0, logit_own, -jnp.inf)
        k_g = k_blocks[b_idx, h_idx, selc]
        v_g = v_blocks[b_idx, h_idx, selc]
        kpos_sel = selc[..., None] * MOBA_BLOCK + offs
        dist_sel = qpos[None, None, :, None, None] - kpos_sel
        bias_sel = bias_t[h_idx[..., None], t5_bucket(dist_sel)]
        logit_sel = jnp.einsum('bhqd,bhqnkd->bhqnk', qc, k_g).astype(jnp.float32) * scale + bias_sel
        logit_sel = jnp.where(validc[None, None, :, :, None], logit_sel, -jnp.inf)
        logits = jnp.concatenate([logit_sel.reshape(B, H, Q_CHUNK, n_sel), logit_own], axis=-1)
        prob = jax.nn.softmax(logits, axis=-1)
        p_sel = prob[..., :n_sel].reshape(B, H, Q_CHUNK, k_sel, MOBA_BLOCK).astype(v.dtype)
        p_own = prob[..., n_sel:].astype(v.dtype)
        return (jnp.einsum('bhqnk,bhqnkd->bhqd', p_sel, v_g)
                + jnp.einsum('bhqk,bhkd->bhqd', p_own, v_own))

    out = lax.map(chunk_fn, (jnp.arange(n_chunks), q_c, sel_c, valid_c))
    out = out.transpose(1, 2, 0, 3, 4).reshape(B, H, s_pad, Dh)
    return out[:, :, :S]

def multiscale_pool(p):
    B, S, G, Cg = p.shape
    pf = p.astype(jnp.float32)
    cs = jnp.concatenate([jnp.zeros((B, 1, G, Cg), jnp.float32), jnp.cumsum(pf, axis=1)], axis=1)
    win = jnp.array(POOL_WINDOWS, jnp.int32)
    t = jnp.arange(S)
    lo = jnp.maximum(t[:, None] + 1 - win[None, :], 0)
    cs_lo = cs[:, lo, jnp.arange(G)[None, :], :]
    count = jnp.minimum(t[:, None] + 1, win[None, :]).astype(jnp.float32)
    mean = (cs[:, 1:] - cs_lo) / count[None, :, :, None]
    return (mean - pf).astype(p.dtype)

def causal_dwconv(u, w, b):
    C = u.shape[-1]
    y = lax.conv_general_dilated(u, w[:, None, :].astype(u.dtype), window_strides=(1,),
                                 padding=((CONV_W - 1, 0),),
                                 dimension_numbers=('NWC', 'WIO', 'NWC'),
                                 feature_group_count=C)
    return y + b

def first_inputs(seed: int = 0) -> dict:
    key = jax.random.key(seed)
    ks = jax.random.split(key, 20)
    L, D = DEPTH, D_MODEL
    nrm = lambda k, shape, s: jax.random.normal(k, shape, jnp.float32) * s
    return {
        "x": nrm(ks[0], (BATCH, SEQ, D), 1.0),
        "c": nrm(ks[1], (BATCH, D), 1.0),
        "ada_w": nrm(ks[2], (L, D, 6 * D), 0.1 * D ** -0.5),
        "ada_b": nrm(ks[3], (L, 6 * D), 0.02),
        "norm1_g": 1.0 + nrm(ks[4], (L, D), 0.05),
        "w_in": nrm(ks[5], (L, D, IN_W), D ** -0.5),
        "q_norm_g": 1.0 + nrm(ks[6], (L, HEAD_DIM), 0.05),
        "k_norm_g": 1.0 + nrm(ks[7], (L, HEAD_DIM), 0.05),
        "rel_bias": nrm(ks[8], (NUM_BUCKETS, ATTN_HEADS), 0.5),
        "pool_w": nrm(ks[9], (L, POOL_GROUPS, POOL_GROUP_W, POOL_GROUP_W), POOL_GROUP_W ** -0.5),
        "pool_scale": 1.0 + nrm(ks[10], (L, POOL_W), 0.1),
        "w_branch_attn": nrm(ks[11], (L, ATTN_W, D), ATTN_W ** -0.5),
        "w_branch_pool": nrm(ks[12], (L, POOL_W, D), POOL_W ** -0.5),
        "w_out": nrm(ks[13], (L, D, D), D ** -0.5),
        "norm2_g": 1.0 + nrm(ks[14], (L, D), 0.05),
        "w_up": nrm(ks[15], (L, D, 2 * D_FF), D ** -0.5),
        "conv_w": nrm(ks[16], (L, CONV_W, 2 * D_FF), CONV_W ** -0.5),
        "conv_b": nrm(ks[17], (L, 2 * D_FF), 0.02),
        "w_down": nrm(ks[18], (L, D_FF, D), D_FF ** -0.5),
    }

def first_block(x, c, ada_w, ada_b, norm1_g, w_in, q_norm_g, k_norm_g, rel_bias, pool_w,
              pool_scale, w_branch_attn, w_branch_pool, w_out, norm2_g, w_up, conv_w, conv_b,
              w_down):
    B, S, D = x.shape
    split_at = [ATTN_W, 2 * ATTN_W, 3 * ATTN_W, 3 * ATTN_W + POOL_W, 3 * ATTN_W + POOL_W + D_MODEL]
    c_act = jax.nn.silu(c)
    for l in range(DEPTH):
        mod = c_act @ ada_w[l] + ada_b[l]
        shift1, scale1, gate1, shift2, scale2, gate2 = [m[:, None, :] for m in jnp.split(mod, 6, axis=-1)]

        h = rms_norm(x, norm1_g[l]) * (1 + scale1) + shift1
        z = h @ w_in[l]
        q, k, v, p, g_attn, g_pool = jnp.split(z, split_at, axis=-1)
        heads = lambda t: t.reshape(B, S, ATTN_HEADS, HEAD_DIM).transpose(0, 2, 1, 3)
        q = rms_norm(heads(q), q_norm_g[l])
        k = rms_norm(heads(k), k_norm_g[l])
        attn = moba_attention(q, k, heads(v), rel_bias)
        attn = attn.transpose(0, 2, 1, 3).reshape(B, S, ATTN_W)
        pool = multiscale_pool(p.reshape(B, S, POOL_GROUPS, POOL_GROUP_W))
        pool = jnp.einsum('bsgc,gcd->bsgd', pool, pool_w[l]).reshape(B, S, POOL_W) * pool_scale[l]
        merged = (jax.nn.sigmoid(g_attn) * (attn @ w_branch_attn[l])
                  + jax.nn.sigmoid(g_pool) * (pool @ w_branch_pool[l]))
        x = x + gate1 * (merged @ w_out[l])

        h2 = rms_norm(x, norm2_g[l]) * (1 + scale2) + shift2
        u = causal_dwconv(h2 @ w_up[l], conv_w[l], conv_b[l])
        u_g, u_v = jnp.split(u, 2, axis=-1)
        x = x + gate2 * ((jax.nn.silu(u_g) * u_v) @ w_down[l])
    return x


DEPTH_2 = 2

D_MIX = D_MODEL
SB_WIDTH = D_MIX // 2
CONV_WIDTH = D_MIX - SB_WIDTH
SB_HEAD_DIM = 64
SB_HEADS = SB_WIDTH // SB_HEAD_DIM
CONV_K = 3
Q_BLOCK = 128
D_FF_2 = 7 * D_MODEL // 2
N_EXPERTS = 8
TOP_K = 2
D_PLE = 256
N_DENSE = (DEPTH_2 + 1) // 2
N_MOE = DEPTH_2 // 2
D_IN_PROJ = 3 * SB_WIDTH + 3 * CONV_WIDTH


def rmsnorm(x, g):
    xf = x.astype(jnp.float32)
    y = xf * lax.rsqrt(jnp.mean(xf * xf, axis=-1, keepdims=True) + EPS)
    return (y * g.astype(jnp.float32)).astype(x.dtype)

def stick_breaking_attention(q, k, v):
    bsz, nh, s_len, dh = q.shape
    dtype = q.dtype
    qf = q.astype(jnp.float32)
    kf = k.astype(jnp.float32)
    vf = v.astype(jnp.float32)
    scale = 1.0 / np.sqrt(dh).astype(np.float32)
    n_blocks = s_len // Q_BLOCK
    q_blocks = qf.reshape(bsz, nh, n_blocks, Q_BLOCK, dh).transpose(2, 0, 1, 3, 4)
    key_pos = jnp.arange(s_len)

    def one_block(args):
        q_blk, blk_idx = args
        z = jnp.einsum('bhqd,bhkd->bhqk', q_blk, kf) * scale
        q_pos = blk_idx * Q_BLOCK + jnp.arange(Q_BLOCK)
        causal = key_pos[None, :] < q_pos[:, None]
        log_beta = jax.nn.log_sigmoid(z)
        log_one_minus = jnp.where(causal, jax.nn.log_sigmoid(-z), 0.0)
        later = lax.cumsum(log_one_minus, axis=3, reverse=True) - log_one_minus
        weights = jnp.where(causal, jnp.exp(log_beta + later), 0.0)
        return jnp.einsum('bhqk,bhkd->bhqd', weights, vf)

    out = lax.map(one_block, (q_blocks, jnp.arange(n_blocks)))
    out = out.transpose(1, 2, 0, 3, 4).reshape(bsz, nh, s_len, dh)
    return out.astype(dtype)

def causal_depthwise_conv(u, w, bias):
    ch = u.shape[-1]
    rhs = w.reshape(CONV_K, 1, ch).astype(u.dtype)
    out = lax.conv_general_dilated(
        u, rhs, window_strides=(1,), padding=[(CONV_K - 1, 0)],
        dimension_numbers=('NWC', 'WIO', 'NWC'), feature_group_count=ch)
    return out + bias.astype(u.dtype)

def swiglu(x, w1, w3, w2):
    return (jax.nn.silu(x @ w1) * (x @ w3)) @ w2

def moe_swiglu(x, router_w, w1, w3, w2):
    bsz, s_len, d = x.shape
    xt = x.reshape(bsz * s_len, d)
    logits = (xt @ router_w).astype(jnp.float32)
    top_vals, top_idx = lax.top_k(logits, TOP_K)
    gates = jax.nn.softmax(top_vals, axis=-1)
    combine = jnp.sum(jax.nn.one_hot(top_idx, N_EXPERTS, dtype=jnp.float32)
                      * gates[..., None], axis=1).astype(x.dtype)
    out = jnp.zeros_like(xt)
    for e in range(N_EXPERTS):
        out = out + combine[:, e:e + 1] * swiglu(xt, w1[e], w3[e], w2[e])
    return out.reshape(bsz, s_len, d)

def second_inputs(seed: int = 0) -> dict:
    key = jax.random.key(seed)
    ks = jax.random.split(key, 24)

    def nrm(k, shape, scale):
        return jax.random.normal(k, shape, jnp.float32) * scale

    def gain(k, shape):
        return 1.0 + 0.02 * jax.random.normal(k, shape, jnp.float32)

    return {
        "x": nrm(ks[0], (BATCH, SEQ, D_MODEL), 1.0),
        "p": nrm(ks[1], (DEPTH_2, BATCH, SEQ, D_PLE), 1.0),
        "mix_norm_g": gain(ks[2], (DEPTH_2, D_MODEL)),
        "w_in": nrm(ks[3], (DEPTH_2, D_MODEL, D_IN_PROJ), D_MODEL ** -0.5),
        "q_norm_g": gain(ks[4], (DEPTH_2, SB_HEAD_DIM)),
        "k_norm_g": gain(ks[5], (DEPTH_2, SB_HEAD_DIM)),
        "conv_w": nrm(ks[6], (DEPTH_2, CONV_K, CONV_WIDTH), CONV_K ** -0.5),
        "conv_b": nrm(ks[7], (DEPTH_2, CONV_WIDTH), 0.02),
        "attn_out_g": gain(ks[8], (DEPTH_2, SB_WIDTH)),
        "conv_out_g": gain(ks[9], (DEPTH_2, CONV_WIDTH)),
        "w_o": nrm(ks[10], (DEPTH_2, D_MIX, D_MODEL), D_MIX ** -0.5),
        "ffn_norm_g": gain(ks[11], (DEPTH_2, D_MODEL)),
        "dense_w1": nrm(ks[12], (N_DENSE, D_MODEL, D_FF_2), D_MODEL ** -0.5),
        "dense_w3": nrm(ks[13], (N_DENSE, D_MODEL, D_FF_2), D_MODEL ** -0.5),
        "dense_w2": nrm(ks[14], (N_DENSE, D_FF_2, D_MODEL), D_FF_2 ** -0.5),
        "router_w": nrm(ks[15], (N_MOE, D_MODEL, N_EXPERTS), D_MODEL ** -0.5),
        "moe_w1": nrm(ks[16], (N_MOE, N_EXPERTS, D_MODEL, D_FF_2), D_MODEL ** -0.5),
        "moe_w3": nrm(ks[17], (N_MOE, N_EXPERTS, D_MODEL, D_FF_2), D_MODEL ** -0.5),
        "moe_w2": nrm(ks[18], (N_MOE, N_EXPERTS, D_FF_2, D_MODEL), D_FF_2 ** -0.5),
        "ple_norm_g": gain(ks[19], (DEPTH_2, D_MODEL)),
        "ple_gate_w": nrm(ks[20], (DEPTH_2, D_MODEL, D_MODEL), D_MODEL ** -0.5),
        "ple_proj_w": nrm(ks[21], (DEPTH_2, D_PLE, D_MODEL), D_PLE ** -0.5),
    }

def second_block(x, p, mix_norm_g, w_in, q_norm_g, k_norm_g, conv_w, conv_b,
              attn_out_g, conv_out_g, w_o, ffn_norm_g, dense_w1, dense_w3, dense_w2,
              router_w, moe_w1, moe_w3, moe_w2, ple_norm_g, ple_gate_w, ple_proj_w):
    bsz, s_len, _ = x.shape
    h = x
    for i in range(DEPTH_2):
        a = rmsnorm(h, mix_norm_g[i])
        proj = a @ w_in[i]
        q, k, v = (proj[..., 0:SB_WIDTH],
                   proj[..., SB_WIDTH:2 * SB_WIDTH],
                   proj[..., 2 * SB_WIDTH:3 * SB_WIDTH])
        off = 3 * SB_WIDTH
        u, c_gate, b_gate = (proj[..., off:off + CONV_WIDTH],
                             proj[..., off + CONV_WIDTH:off + 2 * CONV_WIDTH],
                             proj[..., off + 2 * CONV_WIDTH:off + 3 * CONV_WIDTH])

        def heads(t):
            return t.reshape(bsz, s_len, SB_HEADS, SB_HEAD_DIM).transpose(0, 2, 1, 3)
        qh = rmsnorm(heads(q), q_norm_g[i])
        kh = rmsnorm(heads(k), k_norm_g[i])
        vh = heads(v)
        attn = stick_breaking_attention(qh, kh, vh)
        attn = attn.transpose(0, 2, 1, 3).reshape(bsz, s_len, SB_WIDTH)

        conv = b_gate * causal_depthwise_conv(c_gate * u, conv_w[i], conv_b[i])

        mixed = jnp.concatenate([rmsnorm(attn, attn_out_g[i]),
                                 rmsnorm(conv, conv_out_g[i])], axis=-1)
        h = h + mixed @ w_o[i]

        f = rmsnorm(h, ffn_norm_g[i])
        if i % 2 == 0:
            j = i // 2
            h = h + swiglu(f, dense_w1[j], dense_w3[j], dense_w2[j])
        else:
            j = i // 2
            h = h + moe_swiglu(f, router_w[j], moe_w1[j], moe_w3[j], moe_w2[j])

        gate = jax.nn.sigmoid(rmsnorm(h, ple_norm_g[i]) @ ple_gate_w[i])
        h = h + gate * (p[i] @ ple_proj_w[i])
    return h


def setup_inputs(seed=0):
    out = dict(first_inputs(seed))
    for name, value in second_inputs(seed + 1).items():
        if name != "x":
            out[name + "_2"] = value
    return out


def reference(
    x, c, ada_w, ada_b, norm1_g, w_in, q_norm_g, k_norm_g, rel_bias, pool_w, pool_scale,
    w_branch_attn, w_branch_pool, w_out, norm2_g, w_up, conv_w, conv_b, w_down, p_2,
    mix_norm_g_2, w_in_2, q_norm_g_2, k_norm_g_2, conv_w_2, conv_b_2, attn_out_g_2,
    conv_out_g_2, w_o_2, ffn_norm_g_2, dense_w1_2, dense_w3_2, dense_w2_2, router_w_2, moe_w1_2,
    moe_w3_2, moe_w2_2, ple_norm_g_2, ple_gate_w_2, ple_proj_w_2,
):
    x = first_block(
        x, c, ada_w, ada_b, norm1_g, w_in, q_norm_g, k_norm_g, rel_bias, pool_w, pool_scale,
        w_branch_attn, w_branch_pool, w_out, norm2_g, w_up, conv_w, conv_b, w_down,
    )
    return second_block(
        x, p_2, mix_norm_g_2, w_in_2, q_norm_g_2, k_norm_g_2, conv_w_2, conv_b_2, attn_out_g_2,
        conv_out_g_2, w_o_2, ffn_norm_g_2, dense_w1_2, dense_w3_2, dense_w2_2, router_w_2,
        moe_w1_2, moe_w3_2, moe_w2_2, ple_norm_g_2, ple_gate_w_2, ple_proj_w_2,
    )


_drawn_inputs = setup_inputs


def setup_inputs(seed=0):
    import zlib

    import numpy as np

    out = dict(_drawn_inputs(seed))
    spreads = {}
    factors = {'norm1_g': 8.0,
     'q_norm_g': 8.0,
     'k_norm_g': 8.0,
     'rel_bias': 6.17,
     'pool_scale': 6.363,
     'w_branch_attn': 3.144,
     'norm2_g': 4.312,
     'conv_b': 8.0,
     'q_norm_g_2': 4.929,
     'k_norm_g_2': 7.608,
     'conv_b_2': 2.678,
     'conv_out_g_2': 3.207,
     'ple_norm_g_2': 47.318,
     'attn_out_g_2': 4.669,
     'ffn_norm_g_2': 3.96}
    for name, (base, spread) in spreads.items():
        noise = np.random.default_rng([zlib.crc32(name.encode()), seed]).standard_normal(out[name].shape)
        drawn = base * np.exp(spread * noise) if base else spread * noise
        out[name] = __import__('jax').numpy.asarray(drawn.astype(out[name].dtype))
    for name, factor in factors.items():
        out[name] = (out[name] * factor).astype(out[name].dtype)
    return out
```

```python
from contextlib import ExitStack

import numpy as np
import concourse.bass as bass
from concourse import mybir

ALU = mybir.AluOpType
ACT = mybir.ActivationFunctionType
F32 = mybir.dt.float32
I32 = mybir.dt.int32
AX = mybir.AxisListType.X

P = 128
S = 256
TT = S // P
D = 1024
KD = D // P
HEADS, DH = 8, 64
PAIRS = HEADS // 2
AW = HEADS * DH
CA = AW // P
TRI = S + P
GROUPS = 4
WINDOWS = (2, 4, 8, 16)
BUCKETS, MAX_DISTANCE = 32, 128
FF0 = 2816
FB0 = FF0 // P
FF = 3584
NF = FF // 512
KF = FF // P
EXPERTS = 8
DPLE = 256
EPS = 1e-6
FAR = -1.0e30
RING = 12
UNIT = 2048
UE = 42
CHUNKS = 4

C_ID, C_ANTI, C_GE, C_LT, C_IOTA = (i * P for i in range(5))
C_MASK = 5 * P
C_BAND = C_MASK + TRI
C_RANK = C_BAND + GROUPS * TRI
C_END = C_RANK + EXPERTS
RELV = 512

VROWS = {}
for _name, _n in (("ada_b", 48), ("norm1_g", 8), ("norm2_g", 8), ("c", 8), ("pool_scale", 4),
                  ("conv_w", 132), ("conv_b", 44),
                  ("mix_g", 16), ("ffn_g", 16), ("ple_g", 16), ("attn_g", 8), ("conv_g", 8),
                  ("conv_w2", 24), ("conv_b2", 8), ("qk_g", 6)):
    VROWS[_name] = (sum(n for _, n in VROWS.values()), _n)
NVT = -(-sum(n for _, n in VROWS.values()) // P)


def shape_constants():
    c = np.zeros((P, C_END), np.float32)
    i = np.arange(P)
    c[:, C_ID:C_ID + P] = np.eye(P)
    c[:, C_ANTI:C_ANTI + P] = np.eye(P)[::-1]
    c[:, C_GE:C_GE + P] = i[:, None] >= i[None, :]
    c[:, C_LT:C_LT + P] = i[:, None] < i[None, :]
    c[:, C_IOTA:C_IOTA + P] = i[None, :]
    diag = np.where(i[:, None] < i[None, :], 0.0, FAR)
    c[:, C_MASK:C_MASK + P] = diag
    c[:, C_MASK + S:C_MASK + TRI] = diag
    for g, w in enumerate(WINDOWS):
        s, t = np.arange(S)[:, None], np.arange(S)[None, :]
        count = np.minimum(t + 1, w).astype(np.float32)
        band = np.where((s <= t) & (s > t - w), np.float32(1) / count, 0).astype(np.float32)
        band = (band - (s == t)).astype(np.float32)
        at = C_BAND + g * TRI
        c[:, at:at + S] = band[:P]
        c[:, at + S:at + TRI] = band[P:, P:]
    c[:, C_RANK:C_END] = (EXPERTS - np.arange(EXPERTS))[None, :]
    sel = np.zeros((BUCKETS + 1, RELV), np.float32)
    for m in range(RELV):
        dist = S - 1 - m
        if dist < 0:
            sel[BUCKETS, m] = FAR
            continue
        exact = BUCKETS // 2
        b = dist
        if dist >= exact:
            b = exact + int(np.log(np.float32(dist) / exact) / np.log(MAX_DISTANCE / exact)
                            * (BUCKETS - exact))
        sel[min(b, BUCKETS - 1), m] = 1.0
    return c, sel


class Signal:

    def __init__(self, sem, events):
        self.sem, self.events, self.made = sem, list(events), 0
        self.value = {e: n + 1 for n, e in enumerate(self.events)}

    def mark(self, *event):
        assert self.events[self.made] == event, (self.events[self.made], event)
        self.made += 1
        return self.sem, 1

    def after(self, *event):
        return self.sem, self.value[event]


def weight_stream():
    u = [("ada", pc, q) for pc in (0, 1) for q in range(4)]
    u += [("in", n, kh) for n in range(4) for kh in range(2)] + [("poolw",)]
    for j in range(PAIRS):
        u += [("in", 4 + j, kh) for kh in range(2)]
        u += [("ada", 2 + j, q) for q in range(4)]
    u += [("ba", 0), ("bp", 0), ("ba", 1), ("bp", 1)]
    u += [("out", n, kh) for n in range(2) for kh in range(2)]
    for j in range(FB0 // 2):
        u += [("up", 0, j), ("up", 1, j)]
    u += [("down", t) for t in range(FB0 // 2)]
    for l in (0, 1):
        u += [("in2", l, n, kh) for n in range(3) for kh in range(2)]
        u += [("ucb", l, w, h) for w in range(3) for h in range(2)]
        u += [("pproj", l)]
        u += [("wo", l, n, kh) for n in range(2) for kh in range(2)]
        if l == 0:
            for n in range(NF):
                u += [("d1", n, kh) for kh in range(2)] + [("d3", n, kh) for kh in range(2)]
            u += [("d2", t) for t in range(KF // 2)]
            u += [("pgate", n, kh) for n in range(2) for kh in range(2)]
    return u


def fused_blocks(nc, a, out):
    with ExitStack() as ctx:
        def sb(name, shape, dt=F32):
            return ctx.enter_context(nc.sbuf_tensor(name, shape, dt))

        def sem(name):
            return ctx.enter_context(nc.semaphore(name))

        ring = sb("ring", [P, RING, UNIT])
        h = sb("h", [P, TT, D])
        xn = sb("xn", [P, TT, D])
        aT = sb("aT", [P, KD, S])
        consts = sb("consts", [P, C_END])
        vec = sb("vec", [P, NVT * P])
        pinT = sb("pinT", [P, 2, DPLE // P, S])
        work = sb("work", [P, 17920])
        stat = sb("stat", [P, 256])
        modc = sb("modc", [P, 48])
        acol = sb("acol", [P, 2, KD])
        cact = sb("cact", [P, KD])
        router = sb("router", [P, KD, EXPERTS])
        ones = sb("ones", [P, P])
        epsc = sb("epsc", [P, 1])
        flag = sb("flag", [P, 1], I32)
        slot_of = sb("slot_of", [P, TT, 2 * EXPERTS + 1])
        rel_dram = nc.dram_tensor("bias_by_distance", [HEADS, RELV], F32).ap()

        def wk(lo, *shape):
            n = int(np.prod(shape))
            v = work[:, lo:lo + n]
            if len(shape) == 2:
                return v.rearrange("p (a b) -> p a b", a=shape[0])
            if len(shape) == 3:
                return v.rearrange("p (a b c) -> p a b c", a=shape[0], b=shape[1])
            return v

        qkn = wk(0, 2, TT, AW)
        poolT, poolF = wk(0, CA, S), wk(1024, CA, S)
        qkT = wk(2048, 2, PAIRS, S)
        v = wk(4096, TT, AW)
        pin = wk(5120, TT, GROUPS * P)
        uF = wk(5120, CA, S)
        sc = wk(6144, 2, 2, TRI)
        pr = wk(7680, 2, 2, TRI)
        pT = wk(9216, 2, 2, TRI)
        attnT = wk(10752, CA, S)
        sq = wk(11776, 2, AW)
        biasT = wk(12800, HEADS, TRI)
        cuF, convF, sqF = wk(12800, CA, S), wk(13824, CA, S), wk(14848, CA, S)
        gate_row = wk(12800, D)
        gate_a = wk(15872, TT, D)
        pp = wk(15872, TT, D)
        vrow = wk(0, NVT, P)
        psrc = wk(1024, 2, TT, DPLE)
        relsel = wk(2048, RELV)
        relw = wk(2560, HEADS)
        relv = wk(2600, RELV)
        relrev = wk(9216, HEADS, S)
        gT = wk(0, KF, S)
        g_tmp = wk(7168, 4, 512)
        g_mul = wk(9216, 4, 512)
        cv = wk(7168, 4, 2, S)
        hT = wk(0, KF, P)
        sA = wk(3584, 2, 512)
        hm = wk(4608, 2, 512)
        yg = wk(5632, D)
        pick = wk(6656, TT, P)
        pshare = wk(6912, TT, P)
        shareT = wk(7168, TT, P)
        xgT = aT[:, :, 0:P]
        choice = wk(15616, 8, TT * EXPERTS).rearrange("p k (t e) -> p k t e", t=TT)
        share_of = wk(15776, TT, 2 * EXPERTS + 1)
        pgw = wk(7424, 4, UNIT)
        ident = consts[:, C_ID:C_ID + P]
        anti = consts[:, C_ANTI:C_ANTI + P]
        ge = consts[:, C_GE:C_GE + P]
        before = consts[:, C_LT:C_LT + P]
        iota = consts[:, C_IOTA:C_IOTA + P]
        mask = consts[:, C_MASK:C_MASK + TRI]
        band = consts[:, C_BAND:C_RANK].rearrange("p (g n) -> p g n", g=GROUPS)
        rank = consts[:, C_RANK:C_END]

        def col(name, i):
            return vec[:, VROWS[name][0] + i:VROWS[name][0] + i + 1]

        def cols(name, i, n):
            return vec[:, VROWS[name][0] + i:VROWS[name][0] + i + n]

        main = [ctx.enter_context(nc.psum_tensor(f"main{i}", [P, 512], F32)) for i in range(4)]
        wide = [ctx.enter_context(nc.psum_tensor(n, [P, 1024], F32)) for n in ("X", "Y")]
        bank = main + wide
        X, Y = 4, 5
        filled = [sem(f"filled_{n}") for n in ("m0", "m1", "m2", "m3", "X", "Y")]
        drained = [sem(f"drained_{n}") for n in ("m0", "m1", "m2", "m3", "X", "Y")]
        uses, where = [0] * 6, {}
        turn = [0]

        def bank_open(pe, key, b=None):
            if b is None:
                b = turn[0] % 4
                turn[0] += 1
            if uses[b]:
                pe.wait_ge(drained[b], uses[b])
            uses[b] += 1
            where[key] = (b, uses[b])
            return bank[b]

        def bank_full(ins, key):
            ins.then_inc(filled[where[key][0]], 1)

        def result(eng, key):
            b, n = where[key]
            eng.wait_ge(filled[b], n)
            return bank[b]

        def read_out(ins, key):
            ins.then_inc(drained[where[key][0]], 1)

        def moved(eng, *key):
            b, n = where[key]
            eng.wait_ge(drained[b], n)

        NORMS = range(8)

        def signal(name, events):
            return Signal(sem(name), events)

        loaded = {k: sem(f"loaded_{k}") for k in ("consts", "x", "vrow", "rel", "relrev", "p", "router")}
        rel_stored = sem("rel_stored")
        unit_loaded = [sem(f"unit_loaded_{i}") for i in range(RING)]
        unit_used = sem("unit_used")
        small_set = sem("small_set")
        cact_ready = sem("cact_ready")
        acol_ready = signal("acol_ready", [(0,), (1,)])
        std_ready = signal("std_ready", [(m, tt) for m in NORMS for tt in range(TT)])
        xn_ready = signal("xn_ready", [(m, tt) for m in NORMS for tt in range(TT)])
        QK = [(l, w, tt) for l in range(3) for w in range(2) for tt in range(TT)]
        qk_sq = signal("qk_sq", QK)
        qk_sumsq = signal("qk_sumsq", QK)
        qk_std = signal("qk_std", QK)
        heads0 = [(j,) for j in range(PAIRS)]
        heads12 = [(l, j) for l in (1, 2) for j in range(PAIRS)]
        nmax_ready = signal("nmax_ready", heads0)
        exp_ready = signal("exp_ready", heads0)
        prob_ready = signal("prob_ready", heads0)
        ln_ready = signal("ln_ready", heads12)
        sp_ready = signal("sp_ready", heads12)
        weight_ready = signal("weight_ready", heads12)
        sig_ready = signal("sig_ready", [(0,), (1,)])
        merged_ready = signal("merged_ready", [(n, tt) for n in range(2) for tt in range(TT)])
        h_ready = signal("h_ready", [(m, tt) for m in (1, 2, 5, 7, 8) for tt in range(TT)])
        taps_ready = signal("taps_ready", [(j, half, b) for j in range(FB0 // 2) for half in range(2) for b in range(2)])
        cg_ready = signal("cg_ready", [(j,) for j in range(FB0 // 2)])
        gT_ready = signal("gT_ready", [(j,) for j in range(FB0 // 2)])
        MX = [(l, w) for l in (1, 2) for w in ("conv", "attn")]
        msq_ready = signal("msq_ready", MX)
        mixed_ready = signal("mixed_ready", MX)
        rsF = wk(11776, S)
        psig = wk(3584, 4, 512)
        chosen_ready = sem("chosen_ready")
        margin_ready = sem("margin_ready")
        margin_exp = sem("margin_exp")
        flag_ready = sem("flag_ready")
        e_pick = sem("e_pick")
        e_filled = [sem(f"e_filled_{b}") for b in range(6)]
        e_drained = [sem(f"e_drained_{b}") for b in range(6)]
        e_rows, e_zeroed = sem("e_rows"), sem("e_zeroed")
        last_yg, last_share, last_rows = sem("last_yg"), sem("last_share"), sem("last_rows")
        pgw_loaded = sem("pgw_loaded")
        stored = sem("stored")
        dve_step = sem("dve_step")
        act_step = sem("act_step")

        E_USES = {0: 4, 1: 4, 2: 4, 3: 4, X: 6, Y: 5}

        def e_at(name, n=0):
            if name in ("up", "gate"):
                b = (2 * n + (name == "up")) % 4
                return b, n // 2
            return {"rows": (Y if n else X, 0), "share": (X, 1), "y": (2 + n, 3), "gather": (X, 5),
                    "turn": (X, 2 + n // 2) if n % 2 else (Y, 1 + n // 2)}[name]

        def e_count(i, name, n=0):
            b, k = e_at(name, n)
            return b, i * E_USES[b] + (k + 2)

        units = weight_stream()
        at_unit = {u: n for n, u in enumerate(units)}
        NU = len(units)

        def kn(w, kh, n):
            return w[kh * 512:(kh + 1) * 512, n * 512:(n + 1) * 512].rearrange("(k p) n -> p k n", p=P)

        def k8(w, c0):
            return w[:, c0:c0 + 256].rearrange("(k p) n -> p k n", p=P)

        def k2(w, t):
            return w[t * 256:(t + 1) * 256, :].rearrange("(k p) n -> p k n", p=P)

        def source(u):
            k = u[0]
            if k == "ada":
                return k8(a["ada_w"][0], u[1] * 1024 + u[2] * 256)
            if k == "in":
                return kn(a["w_in"][0], u[2], u[1])
            if k == "poolw":
                return a["pool_w"][0].rearrange("g c d -> c g d")
            if k in ("ba", "bp"):
                return kn(a["w_branch_attn" if k == "ba" else "w_branch_pool"][0], 0, u[1])
            if k == "out":
                return kn(a["w_out"][0], u[2], u[1])
            if k == "up":
                return k8(a["w_up"][0], u[1] * FF0 + u[2] * 256)
            if k == "down":
                return k2(a["w_down"][0], u[1])
            if k == "in2":
                return kn(a["w_in_2"][u[1]], u[3], u[2])
            if k == "ucb":
                return k8(a["w_in_2"][u[1]], 3 * AW + u[2] * 512 + u[3] * 256)
            if k == "pproj":
                return k2(a["ple_proj_w_2"][u[1]], 0)
            if k == "wo":
                return kn(a["w_o_2"][u[1]], u[3], u[2])
            if k == "d1":
                return kn(a["dense_w1_2"][0], u[2], u[1])
            if k == "d3":
                return kn(a["dense_w3_2"][0], u[2], u[1])
            if k == "d2":
                return k2(a["dense_w2_2"][0], u[1])
            return kn(a["ple_gate_w_2"][0], u[2], u[1])

        def slot(n, kc, width):
            return ring[:, n % RING, 0:kc * width].rearrange("p (k n) -> p k n", k=kc)

        block = ctx.enter_context(nc.Block())

        @block.tensor
        def _(pe):
            tr = nc.tensor.transpose
            owed = [0, 0]

            def mm(out, lhsT, rhs, start, stop):
                ins = nc.tensor.matmul(out, lhsT, rhs, start=start, stop=stop)
                if not stop and owed[0] > owed[1]:
                    ins.then_inc(unit_used, owed[0] - owed[1])
                    owed[0] = owed[1]
                return ins

            def free_units(n=1):
                owed[0] += n

            def unit(u, kc, width):
                n = at_unit[u]
                pe.wait_ge(unit_loaded[n % RING], 16 * (n // RING + 1))
                return slot(n, kc, width)

            def norm_turn(m, src=xn):
                for q, b in ((0, X), (1, Y)):
                    o = bank_open(pe, ("norm", m, q), b)
                    o = o[:, :].rearrange("p (c t) -> p c t", t=S)
                    for tt in range(TT):
                        if q == 0:
                            pe.wait_ge(*xn_ready.after(m, tt))
                        for c in range(4):
                            last = tr(o[:, c, tt * P:(tt + 1) * P], src[:, tt, (4 * q + c) * P:(4 * q + c + 1) * P], ident)
                    bank_full(last, ("norm", m, q))

            def wait_aT(kind, m):
                moved(pe, kind, m, 0)
                moved(pe, kind, m, 1)

            def project(name, key):
                outs = [bank_open(pe, (*key, tt)) for tt in range(TT)]
                for kh in range(2):
                    w = unit((*name, kh), 4, 512)
                    for tt in range(TT):
                        for k in range(4):
                            kk = 4 * kh + k
                            last = mm(outs[tt][:, :], aT[:, kk, tt * P:(tt + 1) * P], w[:, k, :],
                                      start=(kk == 0), stop=(kk == KD - 1))
                        if kh == 1:
                            bank_full(last, (*key, tt))
                    free_units()

            def gemv(pc):
                o = bank_open(pe, ("mod", pc))
                for q in range(4):
                    w = unit(("ada", pc, q), 8, 256)
                    for b in range(2):
                        for k in range(KD):
                            last = mm(o[:, 2 * q + b:2 * q + b + 1], w[:, k, b * P:(b + 1) * P],
                                      cact[:, k:k + 1], start=(k == 0), stop=(k == KD - 1))
                    if q == 3:
                        bank_full(last, ("mod", pc))
                    free_units()

            def gate_rows(g):
                moved(pe, "mod", 2 + 3 * g)
                for n in range(2):
                    o = bank_open(pe, ("grow", g, n))
                    for c in range(4):
                        s = modc[:, (2 + 3 * g) * KD + 4 * n + c:(2 + 3 * g) * KD + 4 * n + c + 1]
                        last = mm(o[:, c * P:(c + 1) * P], s.broadcast_to([P, P]), ident, start=True, stop=True)
                    bank_full(last, ("grow", g, n))

            def qk_turn(l, w):
                o = bank_open(pe, ("qkT", l, w), X if w == 0 else Y)
                o = o[:, :].rearrange("p (j t) -> p j t", t=S)
                for tt in range(TT):
                    moved(pe, "qk"[w], l, tt)
                    for j in range(PAIRS):
                        last = tr(o[:, j, tt * P:(tt + 1) * P], qkn[:, w, tt, j * P:(j + 1) * P], ident)
                bank_full(last, ("qkT", l, w))

            def head(x, j, e):
                return x[DH * e:DH * (e + 1), j, :]

            def scores(l, j):
                if j == 0:
                    moved(pe, "qkT", l, 0)
                    moved(pe, "qkT", l, 1)
                o = bank_open(pe, ("score", l, j), X)
                for e in range(2):
                    q, k = head(qkT[:, 0], j, e), head(qkT[:, 1], j, e)
                    at = 512 * e
                    if l == 0:
                        mm(o[:, at:at + S], q[:, P:S], k[:, :], start=True, stop=True)
                        last = mm(o[:, at + S:at + TRI], q[:, 0:P], k[:, 0:P], start=True, stop=True)
                    else:
                        mm(o[:, at:at + S], k[:, 0:P], q[:, :], start=True, stop=True)
                        last = mm(o[:, at + S:at + TRI], k[:, P:S], q[:, P:S], start=True, stop=True)
                bank_full(last, ("score", l, j))

            def prob_turn(j):
                pe.wait_ge(*prob_ready.after(j))
                o = bank_open(pe, ("probT", j), Y)
                for e in range(2):
                    s = pr[:, j % 2, e, :]
                    at = 512 * e
                    tr(o[:, at:at + P], s[:, S:TRI], ident)
                    tr(o[:, at + P:at + S], s[:, 0:P], ident)
                    last = tr(o[:, at + S:at + TRI], s[:, P:S], ident)
                bank_full(last, ("probT", j))

            def later_sums(l, j):
                pe.wait_ge(*sp_ready.after(l, j))
                o = bank_open(pe, ("later", l, j), Y)
                for e in range(2):
                    s = pr[:, j % 2, e, :]
                    at = 512 * e
                    mm(o[:, at + S:at + TRI], ge, s[:, S:TRI], start=True, stop=True)
                    mm(o[:, at:at + S], ge, s[:, 0:S], start=True, stop=False)
                    last = mm(o[:, at + P:at + S], ones[:, :], s[:, S:TRI], start=False, stop=True)
                bank_full(last, ("later", l, j))

            def values(l, j):
                if l == 0:
                    moved(pe, "probT", j)
                else:
                    pe.wait_ge(*weight_ready.after(l, j))
                if j == 0:
                    moved(pe, "v", l, 0)
                    moved(pe, "v", l, 1)
                o = bank_open(pe, ("attn", l, j))
                for e in range(2):
                    hd = 2 * j + e
                    w = pT[:, j % 2, e, :]
                    mm(o[DH * e:DH * (e + 1), 0:S], v[:, 0, hd * DH:(hd + 1) * DH], w[:, 0:S],
                       start=True, stop=False)
                    last = mm(o[DH * e:DH * (e + 1), P:S], v[:, 1, hd * DH:(hd + 1) * DH], w[:, S:TRI],
                              start=False, stop=True)
                bank_full(last, ("attn", l, j))

            def out_rows(name, key):
                ws = [[unit((*name, n, kh), 4, 512) for kh in range(2)] for n in range(2)]
                for tt in range(TT):
                    for n in range(2):
                        o = bank_open(pe, (*key, n, tt))
                        for k in range(KD):
                            last = mm(o[:, :], aT[:, k, tt * P:(tt + 1) * P], ws[n][k // 4][:, k % 4, :],
                                      start=(k == 0), stop=(k == KD - 1))
                        bank_full(last, (*key, n, tt))
                free_units(4)

            def down_rows(name, key, count):
                outs = [[bank_open(pe, (*key, n, tt)) for n in range(2)] for tt in range(TT)]
                for t in range(count):
                    w = unit((*name, t), 2, D)
                    down_wait(name, t)
                    for tt in range(TT):
                        for n in range(2):
                            for k in range(2):
                                kk = 2 * t + k
                                last = mm(outs[tt][n][:, :], gT[:, kk, tt * P:(tt + 1) * P],
                                          w[:, k, n * 512:(n + 1) * 512],
                                          start=(kk == 0), stop=(kk == 2 * count - 1))
                            if t == count - 1:
                                bank_full(last, (*key, n, tt))
                    free_units()

            def down_wait(name, t):
                if name == ("down",):
                    pe.wait_ge(*gT_ready.after(t))
                elif t % 2 == 0:
                    moved(pe, "gT", t // 2)

            pe.wait_ge(loaded["consts"], 16)
            pe.wait_ge(loaded["vrow"], 16)
            o = bank_open(pe, ("vec",), X)
            for t in range(NVT):
                last = tr(o[:, t * P:(t + 1) * P], vrow[:, t, :], ident)
            bank_full(last, ("vec",))
            norm_turn(0)
            pe.wait_ge(loaded["rel"], 32)
            pe.wait_ge(small_set, 3)
            o = bank_open(pe, ("relv",))
            bank_full(mm(o[0:HEADS, :], relw[0:BUCKETS + 1, :], relsel[0:BUCKETS + 1, :], start=True, stop=True), ("relv",))
            pe.wait_ge(loaded["p"], 32)
            for l in range(2):
                o = bank_open(pe, ("pinT", l))
                for k in range(DPLE // P):
                    for tt in range(TT):
                        last = tr(o[:, k * S + tt * P:k * S + (tt + 1) * P], psrc[:, l, tt, k * P:(k + 1) * P], ident)
                bank_full(last, ("pinT", l))
            pe.wait_ge(cact_ready, 1)
            gemv(0)
            gemv(1)
            pe.wait_ge(loaded["relrev"], 16)
            for n in range(4):
                o = bank_open(pe, ("bias", n))
                bank_full(mm(o[:, :], anti, relrev[:, 2 * n:2 * n + 2, :], start=True, stop=True), ("bias", n))

            wait_aT("norm", 0)
            project(("in", 0), ("q", 0))
            project(("in", 1), ("k", 0))
            qk_turn(0, 0)
            project(("in", 2), ("v", 0))
            qk_turn(0, 1)
            project(("in", 3), ("p", 0))
            scores(0, 0)
            for tt in range(TT):
                moved(pe, "p", 0, tt)
            o = bank_open(pe, ("poolT",), Y)
            for g in range(GROUPS):
                mm(o[:, g * S:(g + 1) * S], pin[:, 0, g * P:(g + 1) * P], band[:, g, 0:S], start=True, stop=False)
                last = mm(o[:, g * S + P:(g + 1) * S], pin[:, 1, g * P:(g + 1) * P], band[:, g, S:TRI],
                          start=False, stop=True)
            bank_full(last, ("poolT",))
            for j in range(PAIRS):
                if j == 0:
                    pw = unit(("poolw",), 4, P)
                    moved(pe, "poolT")
                    for g in range(GROUPS):
                        if g % 2 == 0:
                            o = bank_open(pe, ("poolF", g // 2))
                        last = mm(o[:, (g % 2) * S:(g % 2 + 1) * S], pw[:, g, :], poolT[:, g, :], start=True, stop=True)
                        if g % 2:
                            bank_full(last, ("poolF", g // 2))
                    free_units()
                project(("in", 4 + j), ("gate", j))
                gemv(2 + j)
                prob_turn(j)
                if j < PAIRS - 1:
                    scores(0, j + 1)
                values(0, j)
            gate_rows(0)
            for j in range(PAIRS):
                moved(pe, "attn", 0, j)
            moved(pe, "poolF", 0)
            moved(pe, "poolF", 1)
            for n in range(2):
                wa, wp = unit(("ba", n), 4, 512), unit(("bp", n), 4, 512)
                for tt in range(TT):
                    for nm, w, s in (("ba", wa, attnT), ("bp", wp, poolF)):
                        o = bank_open(pe, (nm, n, tt))
                        for k in range(CA):
                            last = mm(o[:, :], s[:, k, tt * P:(tt + 1) * P], w[:, k, :],
                                      start=(k == 0), stop=(k == CA - 1))
                        bank_full(last, (nm, n, tt))
                free_units(2)
            for q, b in ((0, X), (1, Y)):
                o = bank_open(pe, ("merged", 0, q), b)
                o = o[:, :].rearrange("p (c t) -> p c t", t=S)
                for tt in range(TT):
                    pe.wait_ge(*merged_ready.after(q, tt))
                    for c in range(4):
                        last = tr(o[:, c, tt * P:(tt + 1) * P], gate_a[:, tt, (4 * q + c) * P:(4 * q + c + 1) * P], ident)
                bank_full(last, ("merged", 0, q))
            wait_aT("merged", 0)
            out_rows(("out",), ("out", 0))
            gate_rows(1)
            norm_turn(1)
            wait_aT("norm", 1)
            for j in range(FB0 // 2):
                for half in range(2):
                    w = unit(("up", half, j), 8, 256)
                    for b in range(2):
                        o = bank_open(pe, ("up", j, half, b))
                        for k in range(KD):
                            last = mm(o[:, 0:S], w[:, k, b * P:(b + 1) * P], aT[:, k, :],
                                      start=(k == 0), stop=(k == KD - 1))
                        bank_full(last, ("up", j, half, b))
                    free_units()
            down_rows(("down",), ("down", 0), FB0 // 2)

            for l in (1, 2):
                li = l - 1
                m0 = 2 + 3 * li
                norm_turn(m0)
                wait_aT("norm", m0)
                project(("in2", li, 0), ("q", l))
                project(("in2", li, 1), ("k", l))
                qk_turn(l, 0)
                project(("in2", li, 2), ("v", l))
                qk_turn(l, 1)

                def ucb(n):
                    w = unit(("ucb", li, n // 4, (n % 4) // 2), 8, 256)
                    o = bank_open(pe, ("ucb", l, n))
                    for k in range(KD):
                        last = mm(o[:, 0:S], w[:, k, (n % 2) * P:(n % 2 + 1) * P], aT[:, k, :],
                                  start=(k == 0), stop=(k == KD - 1))
                    bank_full(last, ("ucb", l, n))
                    if n % 2:
                        free_units()

                ucb(0)
                scores(l, 0)
                for n in (1, 2, 3):
                    ucb(n)
                for j in range(PAIRS):
                    later_sums(l, j)
                    if j < PAIRS - 1:
                        scores(l, j + 1)
                    if j < PAIRS - 1:
                        for n in ((4, 5, 6), (7, 8, 9), (10, 11))[j]:
                            ucb(n)
                    else:
                        w = unit(("pproj", li), 2, D)
                        for n in range(2):
                            for tt in range(TT):
                                o = bank_open(pe, ("pproj", l, n, tt))
                                for k in range(2):
                                    last = mm(o[:, :], pinT[:, li, k, tt * P:(tt + 1) * P], w[:, k, n * 512:(n + 1) * 512],
                                              start=(k == 0), stop=(k == 1))
                                bank_full(last, ("pproj", l, n, tt))
                        free_units()
                    values(l, j)
                for which in ("conv", "attn"):
                    pe.wait_ge(*msq_ready.after(l, which))
                    o = bank_open(pe, ("mean", l, which))
                    for c in range(CA):
                        last = mm(o[:, 0:S], ones[:, :], sqF[:, c, :], start=(c == 0), stop=(c == CA - 1))
                    bank_full(last, ("mean", l, which))
                pe.wait_ge(*mixed_ready.after(l, "conv"))
                pe.wait_ge(*mixed_ready.after(l, "attn"))
                out_rows(("wo", li), ("wo", l))
                norm_turn(m0 + 1)
                wait_aT("norm", m0 + 1)
                if l == 1:
                    def hidden_turn(n):
                        o = bank_open(pe, ("gT", n), (X, Y)[n % 2])
                        o = o[:, :].rearrange("p (c t) -> p c t", t=S)
                        for tt in range(TT):
                            moved(pe, "d3", n, tt)
                            for c in range(4):
                                last = tr(o[:, c, tt * P:(tt + 1) * P], g_mul[:, 2 * (n % 2) + tt, c * P:(c + 1) * P], ident)
                        bank_full(last, ("gT", n))

                    for n in range(NF):
                        project(("d1", n), ("d1", n))
                        if n:
                            hidden_turn(n - 1)
                        project(("d3", n), ("d3", n))
                    hidden_turn(NF - 1)
                    down_rows(("d2",), ("d2", 0), KF // 2)
                    norm_turn(m0 + 2)
                    wait_aT("norm", m0 + 2)
                    out_rows(("pgate",), ("pgate", l))

            owed[1] = 1
            pe.wait_ge(loaded["router"], 16)
            o = bank_open(pe, ("logits",))
            for tt in range(TT):
                for k in range(KD):
                    last = mm(o[:, tt * EXPERTS:(tt + 1) * EXPERTS], aT[:, k, tt * P:(tt + 1) * P], router[:, k, :],
                              start=(k == 0), stop=(k == KD - 1))
            bank_full(last, ("logits",))
            pe.wait_ge(chosen_ready, 1)
            chosen = choice[:, 6]
            o = bank_open(pe, ("slots",))
            mm(o[:, 0:8], before, chosen[:, 0, :], start=True, stop=True)
            mm(o[:, 8:16], ones[:, :], chosen[:, 0, :], start=True, stop=False)
            mm(o[:, 8:16], before, chosen[:, 1, :], start=False, stop=True)
            mm(o[:, 16:24], ones[:, :], chosen[:, 0, :], start=True, stop=False)
            bank_full(mm(o[:, 16:24], ones[:, :], chosen[:, 1, :], start=False, stop=True), ("slots",))
            for b in range(6):
                pe.wait_ge(drained[b], uses[b])
            for b in (0, 1, 2, 3, Y):
                pe.sem_inc(e_drained[b], 1)
                pe.sem_inc(e_filled[b], 1)

            def gather():
                for c in range(KD):
                    for tt in range(TT):
                        last = mm(wide[0][:, c * P:(c + 1) * P], xn[:, tt, c * P:(c + 1) * P], pick[:, tt, :],
                                  start=(tt == 0), stop=(tt == TT - 1))
                last.then_inc(e_filled[X], 1)

            def scatter(tt):
                for n in range(2):
                    last = mm(wide[tt][:, n * 512:(n + 1) * 512], shareT[:, tt, :], yg[:, n * 512:(n + 1) * 512],
                              start=True, stop=True)
                return last

            def expert(it, odd):
                i = it * 2 + odd

                def take(name, n=0):
                    b, count = e_count(i, name, n)
                    pe.wait_ge(e_drained[b], count - 1)
                    return bank[b]

                def full(ins, name, n=0):
                    ins.then_inc(e_filled[e_at(name, n)[0]], 1)

                def eunit(s, kc, width):
                    n = NU + odd * UE + s
                    pe.wait_ge(unit_loaded[n % RING], it * (16 * 2 * UE // RING) + 16 * (n // RING + 1))
                    return slot(n, kc, width)

                def hidden(s, name, n):
                    o = take(name, n)
                    for kh in range(2):
                        w = eunit(s + kh, 4, 512)
                        for k in range(4):
                            last = mm(o[:, :], xgT[:, 4 * kh + k, :], w[:, k, :], start=(kh + k == 0), stop=(kh * 4 + k == 7))
                        free_units()
                    full(last, name, n)

                def turn(n):
                    b, count = e_count(i, "up", n)
                    pe.wait_ge(e_drained[b], count)
                    o = take("turn", n)
                    for c in range(4):
                        last = tr(o[:, c * P:(c + 1) * P], hm[:, n % 2, c * P:(c + 1) * P], ident)
                    full(last, "turn", n)

                pe.wait_ge(e_drained[X], i * E_USES[X] + 1)
                for n in range(NF):
                    hidden(4 * n, "gate", n)
                    if n == 0:
                        pe.wait_ge(e_drained[2], i * E_USES[2] + 1)
                        pe.wait_ge(e_drained[3], i * E_USES[3] + 1)
                        for tt in range(TT):
                            take("rows", tt)
                            full(scatter(tt), "rows", tt)
                        o = take("share")
                        for tt in range(TT):
                            last = tr(o[:, tt * P:(tt + 1) * P], pshare[:, tt, :], ident)
                        full(last, "share")
                    else:
                        turn(n - 1)
                    hidden(4 * n + 2, "up", n)
                ys = [take("y", 0), take("y", 1)]
                for t in range(KF // 2):
                    w = eunit(4 * NF + t, 2, D)
                    if t % 2 == 0:
                        b, count = e_count(i, "turn", t // 2)
                        pe.wait_ge(e_drained[b], count)
                    for n in range(2):
                        for k in range(2):
                            last = mm(ys[n][:, :], hT[:, 2 * t + k, :], w[:, k, n * 512:(n + 1) * 512],
                                      start=(t + k == 0), stop=(t == KF // 2 - 1 and k == 1))
                        if t == KF // 2 - 1:
                            full(last, "y", n)
                    free_units()
                    if t == 1:
                        turn(NF - 1)
                    if t == 5:
                        pe.wait_ge(e_pick, i + 2)
                        take("gather")
                        gather()

            def passes(first):
                owed[:] = 1, 0
                with pe.Fori(first // 2, first // 2 + EXPERTS // 2) as it:
                    for odd in range(2):
                        expert(it, odd)
                assert owed == [1, 0]

            pe.wait_ge(e_zeroed, 1)
            pe.wait_ge(e_pick, 1)
            gather()
            assert owed == [1, 1]
            passes(0)
            pe.wait_ge(flag_ready, 1)
            over = pe.value_load(flag[0:1, 0:1], min_val=0, max_val=1)
            with pe.If(over == 1):
                passes(EXPERTS)
            pe.wait_ge(last_yg, 1)
            pe.wait_ge(last_share, 1)
            for tt in range(TT):
                scatter(tt).then_inc(last_rows, 1)
            m = 7
            norm_turn(m)
            wait_aT("norm", m)
            pe.wait_ge(pgw_loaded, 64)
            for tt in range(TT):
                for n in range(2):
                    o = bank_open(pe, ("pgate", 2, n, tt))
                    for k in range(KD):
                        w = pgw[:, 2 * n + k // 4, :].rearrange("p (k n) -> p k n", k=4)
                        last = mm(o[:, :], aT[:, k, tt * P:(tt + 1) * P], w[:, k % 4, :], start=(k == 0), stop=(k == KD - 1))
                    bank_full(last, ("pgate", 2, n, tt))

        @block.sync
        def _(sp):
            sp.dma_start(consts[:, :], a["shape_consts"]).then_inc(loaded["consts"], 16)
            for n, u in enumerate(units):
                if n >= RING:
                    sp.wait_ge(unit_used, n - RING + 1)
                src = source(u)
                sp.dma_start(slot(n, src.shape[1], src.shape[2]), src).then_inc(unit_loaded[n % RING], 16)

            def expert_units(it, first):
                for odd in range(2):
                    e = it * 2 + (odd - first)
                    for s in range(UE):
                        n = NU + odd * UE + s
                        sp.wait_ge(unit_used, it * (2 * UE) + (n - RING + 1))
                        if s < 4 * NF:
                            w = a["moe_w1_2" if s % 4 < 2 else "moe_w3_2"][0]
                            src = w[e, (s % 2) * 512:(s % 2 + 1) * 512, (s // 4) * 512:(s // 4 + 1) * 512] \
                                .rearrange("(k p) n -> p k n", p=P)
                        else:
                            t = s - 4 * NF
                            src = a["moe_w2_2"][0][e, t * 256:(t + 1) * 256, :].rearrange("(k p) n -> p k n", p=P)
                        sp.dma_start(slot(n, src.shape[1], src.shape[2]), src).then_inc(unit_loaded[n % RING], 16)

            with sp.Fori(0, EXPERTS // 2) as it:
                expert_units(it, 0)
            sp.wait_ge(flag_ready, 1)
            over = sp.value_load(flag[0:1, 0:1], min_val=0, max_val=1)
            with sp.If(over == 1):
                with sp.Fori(EXPERTS // 2, EXPERTS) as it:
                    expert_units(it, EXPERTS)
            for tt in range(TT):
                sp.wait_ge(*h_ready.after(8, tt))
                sp.dma_start(out[0, tt * P:(tt + 1) * P, :], h[:, tt, :]).then_inc(stored, 16)
            sp.wait_ge(stored, 32)

        @block.gpsimd
        def _(pool):
            pool.dma_start(relw[0:BUCKETS, :], a["rel_bias"]).then_inc(loaded["rel"], 16)
            pool.dma_start(relsel[0:BUCKETS + 1, :], a["shape_buckets"]).then_inc(loaded["rel"], 16)
            for l in range(2):
                pool.dma_start(psrc[:, l], a["p_2"][l, 0].rearrange("(t p) d -> p t d", p=P)).then_inc(loaded["p"], 16)
            pool.dma_start(router[:, :, :], a["router_w_2"][0].rearrange("(k p) e -> p k e", p=P)).then_inc(loaded["router"], 16)
            moved(pool, "relv")
            pool.dma_start(rel_dram, relv[0:HEADS]).then_inc(rel_stored, 16)
            pool.wait_ge(rel_stored, 16)
            rows = bass.AP(tensor=rel_dram.tensor, offset=rel_dram.offset, ap=[[1, P], [RELV, HEADS], [1, S]])
            pool.dma_start(relrev, rows).then_inc(loaded["relrev"], 16)

        def wait_h(eng, m, tt):
            if m in (3, 6):
                for n in range(2):
                    moved(eng, "wo", m // 3, n, tt)
            elif m == 4:
                for n in range(2):
                    moved(eng, "d2", 0, n, tt)
            else:
                eng.wait_ge(*h_ready.after(m, tt))

        def gain_of(m, c):
            return col(("mix_g", "ffn_g", "ple_g")[(m - 2) % 3], (m - 2) // 3 * KD + c)

        @block.scalar
        def _(act):
            fn = nc.scalar.activation
            steps = [0]

            def then(ins):
                ins.then_inc(act_step, 1)
                steps[0] += 1
                act.wait_ge(act_step, steps[0])

            def rms_std(m):
                for tt in range(TT):
                    if m == 0:
                        act.wait_ge(loaded["x"], 16)
                        act.wait_ge(small_set, 3)
                    else:
                        wait_h(act, m, tt)
                    at = 4 * m + 2 * tt
                    then(fn(xn[:, tt, :], h[:, tt, :], ACT.Square, accum_out=stat[:, at:at + 1]))
                    fn(stat[:, at + 1:at + 2], stat[:, at:at + 1], ACT.Sqrt, bias=epsc[:, 0:1],
                       scale=1.0 / D).then_inc(*std_ready.mark(m, tt))

            def norm_out(m):
                o = result(act, ("norm", m, 0))
                for c in range(4):
                    src = o[:, c * S:(c + 1) * S]
                    if m < 2:
                        last = fn(aT[:, c, :], src, ACT.Identity, bias=modc[:, 3 * m * KD + c:3 * m * KD + c + 1],
                                  scale=acol[:, m, c:c + 1])
                    else:
                        last = fn(aT[:, c, :], src, ACT.Copy, scale=gain_of(m, c))
                read_out(last, ("norm", m, 0))

            def qk_stats(l):
                for w in range(2):
                    for tt in range(TT):
                        o = result(act, ("qk"[w], l, tt))
                        fn(sq[:, tt, :], o[:, :], ACT.Square).then_inc(*qk_sq.mark(l, w, tt))
                        act.wait_ge(*qk_sumsq.after(l, w, tt))
                        at = 64 + 16 * (2 * w + tt)
                        fn(stat[:, at + 8:at + 16], stat[:, at:at + 8], ACT.Sqrt, bias=epsc[:, 0:1],
                           scale=1.0 / DH).then_inc(*qk_std.mark(l, w, tt))

            def copy_out(key, dst, n=512, func=ACT.Copy):
                o = result(act, key)
                read_out(fn(dst, o[:, 0:n], func), key)

            def turned(key, dst, n=1024):
                o = result(act, key)
                read_out(fn(dst, o[:, 0:n].rearrange("p (c t) -> p c t", c=4), ACT.Copy), key)

            act.dma_start(h[:, :, :], a["x"][0].rearrange("(t p) d -> p t d", p=P)).then_inc(loaded["x"], 16)
            act.dma_start(vrow, a["vector_rows"].rearrange("(t p) n -> p t n", p=P)).then_inc(loaded["vrow"], 16)
            rms_std(0)
            moved(act, "vec")
            fn(cact[:, :], cols("c", 0, KD), ACT.Silu).then_inc(cact_ready, 1)
            for l in range(2):
                o = result(act, ("pinT", l))
                read_out(fn(pinT[:, l], o[:, :].rearrange("p (k t) -> p k t", t=S), ACT.Copy), ("pinT", l))
            moved(act, "mod", 0)
            act.wait_ge(*acol_ready.after(0))
            norm_out(0)

            qk_stats(0)
            for tt in range(TT):
                copy_out(("v", 0, tt), v[:, tt, :])
            for tt in range(TT):
                copy_out(("p", 0, tt), pin[:, tt, :])
            turned(("poolT",), poolT)
            for j in range(PAIRS):
                act.wait_ge(*nmax_ready.after(j))
                for e in range(2):
                    for part, (lo, hi) in enumerate(((0, S), (S, TRI))):
                        at = 128 + 16 * (j % 2) + 2 * part + e
                        last = fn(pr[:, j % 2, e, lo:hi], sc[:, j % 2, e, lo:hi], ACT.Exp, bias=stat[:, at:at + 1],
                                  accum_out=stat[:, at + 4:at + 5])
                last.then_inc(*exp_ready.mark(j))
                gate = gate_a if j < 2 else xn
                for tt in range(TT):
                    copy_out(("gate", j, tt), gate[:, tt, (j % 2) * 512:(j % 2 + 1) * 512])
                o = result(act, ("probT", j))
                read_out(fn(pT[:, j % 2], o[:, :].rearrange("p (e n) -> p e n", e=2)[:, :, 0:TRI], ACT.Copy), ("probT", j))
            for n in range(2):
                moved(act, "gate", 2 * n + 1, 0)
                moved(act, "gate", 2 * n + 1, 1)
                gate = (gate_a, xn)[n]
                fn(gate[:, :, :], gate[:, :, :], ACT.Sigmoid).then_inc(*sig_ready.mark(n))
            for n in range(2):
                copy_out(("grow", 0, n), gate_row[:, n * 512:(n + 1) * 512])
            turned(("merged", 0, 0), aT[:, 0:4, :])
            rms_std(1)
            for n in range(2):
                copy_out(("grow", 1, n), gate_row[:, n * 512:(n + 1) * 512])
            act.wait_ge(*acol_ready.after(1))
            norm_out(1)
            for j in range(FB0 // 2):
                if j >= 2:
                    act.wait_ge(*gT_ready.after(j - 2))
                for half in range(2):
                    for b in range(2):
                        blk = half * FB0 + 2 * j + b
                        o = result(act, ("up", j, half, b))
                        fn(cv[:, 2 * (j % 2) + half, b, :], o[:, 0:S], ACT.Identity, bias=col("conv_b", blk),
                           scale=col("conv_w", 2 * 2 * FB0 + blk)).then_inc(*taps_ready.mark(j, half, b))
                moved(act, "up", j, 0, 0)
                moved(act, "up", j, 0, 1)
                g = cv[:, 2 * (j % 2), :, :]
                fn(g, g, ACT.Silu).then_inc(*cg_ready.mark(j))

            for l in (1, 2):
                m0 = 2 + 3 * (l - 1)
                rms_std(m0)
                norm_out(m0)
                qk_stats(l)
                for tt in range(TT):
                    copy_out(("v", l, tt), v[:, tt, :])

                def u_out(n):
                    copy_out(("ucb", l, n), uF[:, n, :], S)

                def log_part(j):
                    moved(act, "score", l, j)
                    z, t = sc[:, j % 2], pr[:, j % 2]
                    then(fn(t, z, ACT.Abs))
                    then(fn(t, t, ACT.Exp, scale=-1.0))
                    fn(t, t, ACT.Ln, bias=1.0).then_inc(*ln_ready.mark(l, j))

                u_out(0)
                log_part(0)
                for n in (1, 2, 3):
                    u_out(n)
                for j in range(PAIRS):
                    moved(act, "later", l, j)
                    fn(pT[:, j % 2], sc[:, j % 2], ACT.Exp).then_inc(*weight_ready.mark(l, j))
                    if j < PAIRS - 1:
                        log_part(j + 1)
                for n in range(2):
                    for tt in range(TT):
                        copy_out(("pproj", l, n, tt), pp[:, tt, n * 512:(n + 1) * 512])
                for which, src, last_key in (("conv", convF, ("ucb", l, 11)), ("attn", attnT, ("attn", l, 3))):
                    moved(act, *last_key)
                    if which == "conv":
                        moved(act, "ucb", l, 10)
                        moved(act, "ucb", l, 9)
                        moved(act, "ucb", l, 8)
                    else:
                        for j in range(PAIRS):
                            moved(act, "attn", l, j)
                    fn(sqF, src, ACT.Square).then_inc(*msq_ready.mark(l, which))
                    key = ("mean", l, which)
                    o = result(act, key)
                    if which == "attn":
                        act.wait_ge(*mixed_ready.after(l, "conv"))
                    read_out(fn(rsF, o[:, 0:S], ACT.Sqrt, bias=epsc[:, 0:1], scale=1.0 / AW), key)
                if l == 2:
                    act.wait_ge(*mixed_ready.after(2, "attn"))
                    for n in range(2):
                        for kh in range(2):
                            act.dma_start(pgw[:, 2 * n + kh, :].rearrange("p (k n) -> p k n", k=4),
                                          kn(a["ple_gate_w_2"][1], kh, n)).then_inc(pgw_loaded, 16)
                rms_std(m0 + 1)
                norm_out(m0 + 1)
                if l == 1:
                    for n in range(NF):
                        for tt in range(TT):
                            copy_out(("d1", n, tt), g_tmp[:, 2 * (n % 2) + tt, :], func=ACT.Silu)
                        if n:
                            turned(("gT", n - 1), gT[:, 4 * (n - 1):4 * n, :])
                    turned(("gT", NF - 1), gT[:, 4 * (NF - 1):4 * NF, :])
                    rms_std(m0 + 2)
                    norm_out(m0 + 2)
                    for tt in range(TT):
                        for n in range(2):
                            copy_out(("pgate", l, n, tt), psig[:, 2 * tt + n, :], func=ACT.Sigmoid)

            act.wait_ge(margin_ready, 1)
            fn(stat[:, 172:174], stat[:, 170:172], ACT.Exp).then_inc(margin_exp, 1)

            def expert(i):
                def e_result(name, n=0):
                    b, count = e_count(i, name, n)
                    act.wait_ge(e_filled[b], count)
                    return bank[b], e_drained[b]

                def turned_h(n):
                    o, free = e_result("turn", n)
                    fn(hT[:, 4 * n:4 * n + 4, :], o[:, 0:512].rearrange("p (c t) -> p c t", c=4), ACT.Copy).then_inc(free, 1)

                for n in range(NF):
                    o, free = e_result("gate", n)
                    fn(sA[:, n % 2, :], o[:, :], ACT.Silu).then_inc(free, 1)
                    if n:
                        turned_h(n - 1)
                turned_h(NF - 1)
                for n in range(2):
                    o, free = e_result("y", n)
                    fn(yg[:, n * 512:(n + 1) * 512], o[:, :], ACT.Copy).then_inc(free, 1)

            def passes(first):
                with act.Fori(first // 2, first // 2 + EXPERTS // 2) as it:
                    for odd in range(2):
                        expert(it * 2 + odd)
                for b in (2, 3):
                    act.wait_ge(e_drained[b], (first + EXPERTS) * E_USES[b] + 1)

            passes(0)
            act.wait_ge(flag_ready, 1)
            over = act.value_load(flag[0:1, 0:1], min_val=0, max_val=1)
            with act.If(over == 1):
                passes(EXPERTS)
            act.sem_inc(last_yg, 1)
            rms_std(7)
            norm_out(7)
            for tt in range(TT):
                for n in range(2):
                    copy_out(("pgate", 2, n, tt), psig[:, 2 * tt + n, :], func=ACT.Sigmoid)

        @block.vector
        def _(dve):
            V = nc.vector
            steps = [0]

            def then(ins):
                ins.then_inc(dve_step, 1)
                steps[0] += 1
                dve.wait_ge(dve_step, steps[0])

            def normalise(m):
                for tt in range(TT):
                    dve.wait_ge(*std_ready.after(m, tt))
                    at = 4 * m + 2 * tt + 1
                    r = stat[:, 32 + 2 * m + tt:33 + 2 * m + tt]
                    then(V.reciprocal(r, stat[:, at:at + 1]))
                    V.tensor_scalar(xn[:, tt, :], h[:, tt, :], r, None, ALU.mult).then_inc(*xn_ready.mark(m, tt))

            def norm_out(m):
                o = result(dve, ("norm", m, 1))
                for c in range(4, KD):
                    src = o[:, (c - 4) * S:(c - 3) * S]
                    if m < 2:
                        last = V.tensor_scalar(aT[:, c, :], src, acol[:, m, c:c + 1],
                                               modc[:, 3 * m * KD + c:3 * m * KD + c + 1], ALU.mult, ALU.add)
                    else:
                        last = V.tensor_scalar(aT[:, c, :], src, gain_of(m, c), None, ALU.mult)
                read_out(last, ("norm", m, 1))

            def modulation(pc):
                o = result(dve, ("mod", pc))
                read_out(V.tensor_tensor(modc[:, pc * KD:(pc + 1) * KD], o[:, 0:KD], cols("ada_b", pc * KD, KD), ALU.add),
                         ("mod", pc))
                if pc in (1, 4):
                    moved(dve, "mod", pc)
                    g = pc // 3
                    V.scalar_tensor_tensor(out=acol[:, g, :], in0=modc[:, pc * KD:(pc + 1) * KD], scalar=1.0,
                                           in1=cols(("norm1_g", "norm2_g")[g], 0, KD), op0=ALU.add,
                                           op1=ALU.mult).then_inc(*acol_ready.mark(g))

            def qk_norm(l):
                for w in range(2):
                    for tt in range(TT):
                        at = 64 + 16 * (2 * w + tt)
                        dve.wait_ge(*qk_sq.after(l, w, tt))
                        V.reduce_sum(stat[:, at:at + 8], sq[:, tt, :].rearrange("p (h d) -> p h d", d=DH),
                                     AX).then_inc(*qk_sumsq.mark(l, w, tt))
                        dve.wait_ge(*qk_std.after(l, w, tt))
                        r = stat[:, 136 + 24:136 + 32]
                        then(V.reciprocal(r, stat[:, at + 8:at + 16]))
                        key = ("qk"[w], l, tt)
                        o = result(dve, key)
                        read_out(V.tensor_tensor(qkn[:, w, tt, :].rearrange("p (h d) -> p h d", d=DH),
                                                 o[:, :].rearrange("p (h d) -> p h d", d=DH),
                                                 r[:, :, None].broadcast_to([P, HEADS, DH]), ALU.mult), key)
                for w in range(2):
                    key = ("qkT", l, w)
                    o = result(dve, key)
                    read_out(V.tensor_scalar(qkT[:, w], o[:, :].rearrange("p (j t) -> p j t", t=S), col("qk_g", 2 * l + w),
                                             DH ** -0.5 if w == 0 else 1.0, ALU.mult, ALU.mult), key)

            def attn_out(l, j):
                key = ("attn", l, j)
                o = result(dve, key)
                read_out(V.tensor_copy(attnT[:, j, :], o[:, 0:S]), key)

            def pair(x, lo=0, hi=TRI):
                return x[:, :].rearrange("p (e n) -> p e n", e=2)[:, :, lo:hi]

            def turned(key, dst):
                o = result(dve, key)
                read_out(V.tensor_copy(dst, o[:, :].rearrange("p (c t) -> p c t", c=4)), key)

            V.memset(epsc[:, :], EPS).then_inc(small_set, 1)
            V.memset(ones[:, :], 1.0).then_inc(small_set, 1)
            V.memset(relw[BUCKETS:BUCKETS + 1, :], 1.0).then_inc(small_set, 1)
            normalise(0)
            o = result(dve, ("vec",))
            read_out(V.tensor_copy(vec[:, :], o[:, 0:NVT * P]), ("vec",))
            o = result(dve, ("relv",))
            read_out(V.tensor_copy(relv[0:HEADS], o[0:HEADS, :]), ("relv",))
            moved(dve, "vec")
            modulation(0)
            modulation(1)
            moved(dve, "mod", 0)
            dve.wait_ge(*acol_ready.after(0))
            norm_out(0)
            for n in range(4):
                o = result(dve, ("bias", n))
                s = o[:, :].rearrange("p (e k) -> p e k", e=2)
                V.tensor_copy(biasT[:, 2 * n:2 * n + 2, 0:S], s)
                read_out(V.tensor_copy(biasT[:, 2 * n:2 * n + 2, S:TRI], s[:, :, P:S]), ("bias", n))

            qk_norm(0)
            for n in range(4):
                moved(dve, "bias", n)

            def biased_scores(j):
                o = result(dve, ("score", 0, j))
                s = sc[:, j % 2]
                read_out(V.tensor_tensor(s, pair(o), biasT[:, 2 * j:2 * j + 2, :], ALU.add), ("score", 0, j))
                moved(dve, "score", 0, j)
                at = 128 + 16 * (j % 2)
                V.reduce_max(stat[:, at + 8:at + 10], s[:, :, 0:S], AX)
                then(V.reduce_max(stat[:, at + 10:at + 12], s[:, :, S:TRI], AX))
                V.tensor_scalar(stat[:, at:at + 4], stat[:, at + 8:at + 12], -1.0, None, ALU.mult)\
                    .then_inc(*nmax_ready.mark(j))

            def probabilities(j):
                dve.wait_ge(*exp_ready.after(j))
                at = 128 + 16 * (j % 2)
                then(V.reciprocal(stat[:, at + 12:at + 16], stat[:, at + 4:at + 8]))
                p = pr[:, j % 2]
                V.tensor_tensor(p[:, :, 0:S], p[:, :, 0:S], stat[:, at + 12:at + 14, None].broadcast_to([P, 2, S]), ALU.mult)
                V.tensor_tensor(p[:, :, S:TRI], p[:, :, S:TRI], stat[:, at + 14:at + 16, None].broadcast_to([P, 2, P]),
                                ALU.mult).then_inc(*prob_ready.mark(j))

            biased_scores(0)
            for g in range(2):
                key = ("poolF", g)
                o = result(dve, key)
                read_out(V.tensor_tensor(poolF[:, 2 * g:2 * g + 2, :], o[:, :].rearrange("p (g t) -> p g t", g=2),
                                         cols("pool_scale", 2 * g, 2)[:, :, None].broadcast_to([P, 2, S]), ALU.mult), key)
            for j in range(PAIRS):
                probabilities(j)
                modulation(2 + j)
                if j < PAIRS - 1:
                    biased_scores(j + 1)
                attn_out(0, j)
            for n in range(2):
                dve.wait_ge(*sig_ready.after(n))
            for n in range(2):
                for tt in range(TT):
                    ga, gp = (g[:, tt, n * 512:(n + 1) * 512] for g in (gate_a, xn))
                    for nm, g in (("ba", ga), ("bp", gp)):
                        o = result(dve, (nm, n, tt))
                        read_out(V.tensor_tensor(g, g, o[:, :], ALU.mult), (nm, n, tt))
                    moved(dve, "ba", n, tt)
                    moved(dve, "bp", n, tt)
                    V.tensor_tensor(ga, ga, gp, ALU.add).then_inc(*merged_ready.mark(n, tt))
            turned(("merged", 0, 1), aT[:, 4:8, :])

            def gated_rows(name, m):
                for tt in range(TT):
                    for n in range(2):
                        key = (name, 0, n, tt)
                        o = result(dve, key)
                        t = sq[:, n, :]
                        hh = h[:, tt, n * 512:(n + 1) * 512]
                        read_out(V.tensor_tensor(t, o[:, :], gate_row[:, n * 512:(n + 1) * 512], ALU.mult), key)
                        moved(dve, *key)
                        last = V.tensor_tensor(hh, hh, t, ALU.add)
                        if n == 0:
                            then(last)
                    last.then_inc(*h_ready.mark(m, tt))

            for n in range(2):
                moved(dve, "grow", 0, n)
            gated_rows("out", 1)
            normalise(1)
            dve.wait_ge(*acol_ready.after(1))
            norm_out(1)
            for j in range(FB0 // 2):
                for half in range(2):
                    for b in range(2):
                        blk = half * FB0 + 2 * j + b
                        key = ("up", j, half, b)
                        o = result(dve, key)
                        dve.wait_ge(*taps_ready.after(j, half, b))
                        y = cv[:, 2 * (j % 2) + half, b, :]
                        then(V.scalar_tensor_tensor(out=y[:, 1:S], in0=o[:, 0:S - 1], scalar=col("conv_w", 2 * FB0 + blk),
                                                    in1=y[:, 1:S], op0=ALU.mult, op1=ALU.add))
                        read_out(V.scalar_tensor_tensor(out=y[:, 2:S], in0=o[:, 0:S - 2], scalar=col("conv_w", blk),
                                                        in1=y[:, 2:S], op0=ALU.mult, op1=ALU.add), key)
                dve.wait_ge(*cg_ready.after(j))
                moved(dve, "up", j, 1, 0)
                moved(dve, "up", j, 1, 1)
                V.tensor_tensor(gT[:, 2 * j:2 * j + 2, :], cv[:, 2 * (j % 2)], cv[:, 2 * (j % 2) + 1], ALU.mult)\
                    .then_inc(*gT_ready.mark(j))
            for n in range(2):
                moved(dve, "grow", 1, n)
            gated_rows("down", 2)

            def add_rows(name, l):
                for tt in range(TT):
                    for n in range(2):
                        key = (name, l, n, tt)
                        o = result(dve, key)
                        hh = h[:, tt, n * 512:(n + 1) * 512]
                        read_out(V.tensor_tensor(hh, hh, o[:, :], ALU.add), key)

            def gate_ple(l, m):
                for tt in range(TT):
                    for n in range(2):
                        key = ("pgate", l, n, tt)
                        moved(dve, *key)
                        t = psig[:, 2 * tt + n, :]
                        hh = h[:, tt, n * 512:(n + 1) * 512]
                        then(V.tensor_tensor(t, t, pp[:, tt, n * 512:(n + 1) * 512], ALU.mult))
                        last = V.tensor_tensor(hh, hh, t, ALU.add)
                        if n == 0:
                            then(last)
                    last.then_inc(*h_ready.mark(m, tt))

            for l in (1, 2):
                li = l - 1
                m0 = 2 + 3 * li
                normalise(m0)
                norm_out(m0)
                qk_norm(l)

                def masked_scores(j):
                    key = ("score", l, j)
                    o = result(dve, key)
                    read_out(V.tensor_tensor(sc[:, j % 2], pair(o), mask[:, None, :].broadcast_to([P, 2, TRI]), ALU.add), key)

                def softplus(j):
                    dve.wait_ge(*ln_ready.after(l, j))
                    V.scalar_tensor_tensor(out=pr[:, j % 2], in0=sc[:, j % 2], scalar=0.0, in1=pr[:, j % 2],
                                           op0=ALU.max, op1=ALU.add).then_inc(*sp_ready.mark(l, j))

                def ucb(n):
                    b = n % 4
                    key = ("ucb", l, n)
                    if n < 8:
                        moved(dve, "ucb", l, b)
                        o = result(dve, key)
                        read_out(V.tensor_tensor(cuF[:, b, :], o[:, 0:S], uF[:, b, :], ALU.mult), key)
                        moved(dve, *key)
                        y, x = convF[:, b, :], cuF[:, b, :]
                        tap = [col("conv_w2", 12 * li + 4 * t + b) for t in range(3)]
                        then(V.tensor_scalar(y, x, tap[2], col("conv_b2", 4 * li + b), ALU.mult, ALU.add))
                        then(V.scalar_tensor_tensor(out=y[:, 1:S], in0=x[:, 0:S - 1], scalar=tap[1], in1=y[:, 1:S],
                                                    op0=ALU.mult, op1=ALU.add))
                        then(V.scalar_tensor_tensor(out=y[:, 2:S], in0=x[:, 0:S - 2], scalar=tap[0], in1=y[:, 2:S],
                                                    op0=ALU.mult, op1=ALU.add))
                    else:
                        o = result(dve, key)
                        read_out(V.tensor_tensor(convF[:, b, :], convF[:, b, :], o[:, 0:S], ALU.mult), key)

                masked_scores(0)
                softplus(0)
                for j in range(PAIRS):
                    key = ("later", l, j)
                    o = result(dve, key)
                    read_out(V.tensor_tensor(sc[:, j % 2], sc[:, j % 2], pair(o), ALU.subtract), key)
                    if j < PAIRS - 1:
                        masked_scores(j + 1)
                        softplus(j + 1)
                        for n in ((4, 5, 6), (7, 8, 9), (10, 11))[j]:
                            ucb(n)
                    attn_out(l, j)
                for which, src, at, gname in (("conv", convF, 4, "conv_g"), ("attn", attnT, 0, "attn_g")):
                    moved(dve, "mean", l, which)
                    then(V.reciprocal(rsF, rsF))
                    for c in range(CA):
                        last = V.scalar_tensor_tensor(out=aT[:, at + c, :], in0=src[:, c, :], scalar=col(gname, 4 * li + c),
                                                      in1=rsF, op0=ALU.mult, op1=ALU.mult)
                    last.then_inc(*mixed_ready.mark(l, which))
                add_rows("wo", l)
                normalise(m0 + 1)
                norm_out(m0 + 1)
                if l == 1:
                    for n in range(NF):
                        for tt in range(TT):
                            moved(dve, "d1", n, tt)
                            key = ("d3", n, tt)
                            o = result(dve, key)
                            read_out(V.tensor_tensor(g_mul[:, 2 * (n % 2) + tt, :], g_tmp[:, 2 * (n % 2) + tt, :], o[:, :],
                                                     ALU.mult), key)
                    add_rows("d2", 0)
                    normalise(m0 + 2)
                    norm_out(m0 + 2)
                    gate_ple(1, 5)

            LG, LG2, EQ, ONE1, ONE2, SH, CHO, T = (choice[:, k] for k in range(8))
            rankb = rank[:, None, :].broadcast_to([P, TT, EXPERTS])

            def spread(x):
                return x[:, :, None].broadcast_to([P, TT, EXPERTS])

            o = result(dve, ("logits",))
            read_out(V.tensor_copy(LG, o[:, 0:16].rearrange("p (t e) -> p t e", t=TT)), ("logits",))
            moved(dve, "logits")
            for lg, one, top in ((LG, ONE1, stat[:, 180:182]), (LG2, ONE2, stat[:, 182:184])):
                then(V.reduce_max(top, lg, AX))
                then(V.tensor_tensor(EQ, lg, spread(top), ALU.is_equal))
                then(V.tensor_tensor(EQ, EQ, rankb, ALU.mult))
                then(V.reduce_max(stat[:, 184:186], EQ, AX))
                then(V.tensor_tensor(one, spread(stat[:, 184:186]), rankb, ALU.is_equal))
                if lg is LG:
                    then(V.scalar_tensor_tensor(out=LG2, in0=one, scalar=FAR, in1=LG, op0=ALU.mult, op1=ALU.add))
            V.tensor_tensor(stat[:, 170:172], stat[:, 182:184], stat[:, 180:182], ALU.subtract).then_inc(margin_ready, 1)
            V.tensor_tensor(CHO, ONE1, ONE2, ALU.add).then_inc(chosen_ready, 1)
            dve.wait_ge(margin_exp, 1)
            then(V.tensor_scalar(stat[:, 174:176], stat[:, 172:174], 1.0, None, ALU.add))
            then(V.reciprocal(stat[:, 176:178], stat[:, 174:176]))
            then(V.tensor_tensor(stat[:, 178:180], stat[:, 172:174], stat[:, 176:178], ALU.mult))
            then(V.tensor_tensor(ONE1, ONE1, spread(stat[:, 176:178]), ALU.mult))
            then(V.tensor_tensor(ONE2, ONE2, spread(stat[:, 178:180]), ALU.mult))
            then(V.memset(share_of[:, :, :], 0.0))
            V.tensor_tensor(share_of[:, :, 0:8], ONE1, ONE2, ALU.add)
            then(V.tensor_tensor(share_of[:, :, 8:16], ONE1, ONE2, ALU.add))
            then(V.memset(slot_of[:, :, :], -1.0))
            o = result(dve, ("slots",))
            then(V.scalar_tensor_tensor(out=T, in0=o[:, 0:16].rearrange("p (t e) -> p t e", t=TT), scalar=1.0, in1=CHO,
                                        op0=ALU.add, op1=ALU.mult))
            V.tensor_scalar(slot_of[:, :, 0:8], T, -1.0, None, ALU.add)
            then(V.tensor_scalar(slot_of[:, :, 8:16], T, -1.0 - P, None, ALU.add))
            then(V.reduce_max(stat[:, 190:191], o[:, 16:24], AX))
            read_out(V.tensor_scalar(flag[:, 0:1], stat[:, 190:191], float(P), None, ALU.is_gt), ("slots",))
            moved(dve, "slots")
            dve.sem_inc(flag_ready, 1)

            def pick_tokens(i):
                for tt in range(TT):
                    V.tensor_scalar(pshare[:, tt, :], iota, slot_of[:, tt, bass.ds(i, 1)], share_of[:, tt, bass.ds(i, 1)],
                                    ALU.is_equal, ALU.mult)
                for tt in range(TT):
                    last = V.tensor_scalar(pick[:, tt, :], iota, slot_of[:, tt, bass.ds(i, 1)], None, ALU.is_equal)
                last.then_inc(e_pick, 1)

            def gathered():
                return V.tensor_tensor(xgT, wide[0][:, :].rearrange("p (c t) -> p c t", t=P),
                                       cols("ffn_g", KD, KD)[:, :, None].broadcast_to([P, KD, P]), ALU.mult)

            V.memset(yg, 0.0).then_inc(e_zeroed, 1)
            V.memset(shareT, 0.0).then_inc(e_zeroed, 1)
            pick_tokens(0)
            dve.wait_ge(e_filled[X], 1)
            gathered().then_inc(e_drained[X], 1)

            def expert(i):
                def e_result(name, n=0):
                    b, count = e_count(i, name, n)
                    dve.wait_ge(e_filled[b], count)
                    return bank[b], e_drained[b]

                for tt in range(TT):
                    o, free = e_result("rows", tt)
                    V.tensor_tensor(h[:, tt, :], h[:, tt, :], o[:, :], ALU.add).then_inc(free, 1)
                o, free = e_result("share")
                V.tensor_copy(shareT, o[:, 0:S].rearrange("p (t s) -> p t s", t=TT)).then_inc(free, 1)
                pick_tokens(i + 1)
                for n in range(NF):
                    b, count = e_count(i, "gate", n)
                    dve.wait_ge(e_drained[b], count)
                    o, free = e_result("up", n)
                    V.tensor_tensor(hm[:, n % 2, :], sA[:, n % 2, :], o[:, :], ALU.mult).then_inc(free, 1)
                o, free = e_result("gather")
                gathered().then_inc(free, 1)

            def passes(first):
                with dve.Fori(first // 2, first // 2 + EXPERTS // 2) as it:
                    for odd in range(2):
                        expert(it * 2 + odd)
                dve.wait_ge(e_drained[X], (first + EXPERTS) * E_USES[X] + 1)
                dve.wait_ge(e_drained[Y], (first + EXPERTS) * E_USES[Y] + 1)

            passes(0)
            over = dve.value_load(flag[0:1, 0:1], min_val=0, max_val=1)
            with dve.If(over == 1):
                passes(EXPERTS)
            dve.sem_inc(last_share, 1)
            for tt in range(TT):
                dve.wait_ge(last_rows, tt + 1)
                V.tensor_tensor(h[:, tt, :], h[:, tt, :], wide[tt][:, :], ALU.add).then_inc(*h_ready.mark(7, tt))
            normalise(7)
            norm_out(7)
            gate_ple(2, 8)


_NAMES = ['x', 'ada_w', 'w_in', 'rel_bias', 'pool_w', 'w_branch_attn', 'w_branch_pool', 'w_out', 'w_up', 'w_down',
          'p_2', 'w_in_2', 'w_o_2', 'dense_w1_2', 'dense_w3_2', 'dense_w2_2', 'router_w_2', 'moe_w1_2', 'moe_w3_2',
          'moe_w2_2', 'ple_gate_w_2', 'ple_proj_w_2', 'vector_rows', 'shape_consts', 'shape_buckets']


def kernel(**inputs):
    import concourse.bacc as _bacc
    from concourse.bass_utils import run_bass_kernel_spmd as _run

    given = {k: np.ascontiguousarray(v) for k, v in inputs.items()}
    gains = [np.tile(given[n][l], 2) for n, l in (("q_norm_g", 0), ("k_norm_g", 0), ("q_norm_g_2", 0),
                                                 ("k_norm_g_2", 0), ("q_norm_g_2", 1), ("k_norm_g_2", 1))]
    rows = {"ada_b": given["ada_b"], "norm1_g": given["norm1_g"], "norm2_g": given["norm2_g"], "c": given["c"],
            "pool_scale": given["pool_scale"], "conv_w": given["conv_w"], "conv_b": given["conv_b"],
            "mix_g": given["mix_norm_g_2"], "ffn_g": given["ffn_norm_g_2"], "ple_g": given["ple_norm_g_2"],
            "attn_g": given["attn_out_g_2"], "conv_g": given["conv_out_g_2"], "conv_w2": given["conv_w_2"],
            "conv_b2": given["conv_b_2"], "qk_g": np.stack(gains)}
    rows = [rows[n].reshape(-1, P) for n in VROWS]
    rows.append(np.zeros((NVT * P - sum(len(r) for r in rows), P), np.float32))
    given["vector_rows"] = np.concatenate(rows)
    given["shape_consts"], given["shape_buckets"] = shape_constants()

    nc = _bacc.Bacc("TRN2", target_bir_lowering=False, num_devices=1)
    arrays, args = {}, {}
    for name in _NAMES:
        v = given[name]
        arrays[f"in_{name}"] = v
        args[name] = nc.dram_tensor(f"in_{name}", v.shape, mybir.dt.from_np(v.dtype), kind="ExternalInput").ap()
    out = nc.dram_tensor("out", (1, S, D), F32, kind="ExternalOutput").ap()
    fused_blocks(nc, args, out)
    r = _run(nc, [arrays], core_ids=[0])
    return r.results[0]["out"]
```

```python
from contextlib import ExitStack

import numpy as np
import concourse.bass as bass
from concourse import mybir

ALU = mybir.AluOpType
ACT = mybir.ActivationFunctionType
F32 = mybir.dt.float32
F32R = mybir.dt.float32r
I32 = mybir.dt.int32
AX = mybir.AxisListType.X

P = 128
S = 256
TT = S // P
D = 1024
KD = D // P
HEADS, DH = 8, 64
PAIRS = HEADS // 2
AW = HEADS * DH
CA = AW // P
TRI = S + P
GROUPS = 4
WINDOWS = (2, 4, 8, 16)
BUCKETS, MAX_DISTANCE = 32, 128
FF0 = 2816
FB0 = FF0 // P
FF = 3584
NF = FF // 512
KF = FF // P
EXPERTS = 8
DPLE = 256
EPS = 1e-6
FAR = -1.0e30
RAW = 4
HALF = 3
ARENA = 19600
UNIT = 2048
UE = 42
CHUNKS = 4

C_ID, C_ANTI, C_GE, C_LT, C_IOTA = (i * P for i in range(5))
C_MASK = 5 * P
C_BAND = C_MASK + TRI
C_RANK = C_BAND + GROUPS * TRI
C_END = C_RANK + EXPERTS
RELV = 512

VROWS = {}
for _name, _n in (("ada_b", 48), ("norm1_g", 8), ("norm2_g", 8), ("c", 8), ("pool_scale", 4),
                  ("conv_w", 132), ("conv_b", 44),
                  ("mix_g", 16), ("ffn_g", 16), ("ple_g", 16), ("attn_g", 8), ("conv_g", 8),
                  ("conv_w2", 24), ("conv_b2", 8), ("qk_g", 6)):
    VROWS[_name] = (sum(n for _, n in VROWS.values()), _n)
NVT = -(-sum(n for _, n in VROWS.values()) // P)


def shape_constants():
    c = np.zeros((P, C_END), np.float32)
    i = np.arange(P)
    c[:, C_ID:C_ID + P] = np.eye(P)
    c[:, C_ANTI:C_ANTI + P] = np.eye(P)[::-1]
    c[:, C_GE:C_GE + P] = i[:, None] >= i[None, :]
    c[:, C_LT:C_LT + P] = i[:, None] < i[None, :]
    c[:, C_IOTA:C_IOTA + P] = i[None, :]
    diag = np.where(i[:, None] < i[None, :], 0.0, FAR)
    c[:, C_MASK:C_MASK + P] = diag
    c[:, C_MASK + S:C_MASK + TRI] = diag
    for g, w in enumerate(WINDOWS):
        s, t = np.arange(S)[:, None], np.arange(S)[None, :]
        count = np.minimum(t + 1, w).astype(np.float32)
        band = np.where((s <= t) & (s > t - w), np.float32(1) / count, 0).astype(np.float32)
        band = (band - (s == t)).astype(np.float32)
        at = C_BAND + g * TRI
        c[:, at:at + S] = band[:P]
        c[:, at + S:at + TRI] = band[P:, P:]
    c[:, C_RANK:C_END] = (EXPERTS - np.arange(EXPERTS))[None, :]
    sel = np.zeros((BUCKETS + 1, RELV), np.float32)
    for m in range(RELV):
        dist = S - 1 - m
        if dist < 0:
            sel[BUCKETS, m] = FAR
            continue
        exact = BUCKETS // 2
        b = dist
        if dist >= exact:
            b = exact + int(np.log(np.float32(dist) / exact) / np.log(MAX_DISTANCE / exact)
                            * (BUCKETS - exact))
        sel[min(b, BUCKETS - 1), m] = 1.0
    return c, sel


HI_STEPS = [("norm", 0, q) for q in range(4)] + [("merged", 0, q) for q in range(4)]
HI_STEPS += [("norm", 1, q) for q in range(4)] + [("g", 0, j) for j in range(FB0 // 2)]
HI_STEPS += [("norm", m, q) for m in (2, 3) for q in range(4)] + [("gT", n, q) for n in range(NF) for q in range(2)]
HI_STEPS += [("norm", m, q) for m in (4, 5, 6, 7) for q in range(4)]


class Signal:

    def __init__(self, sem, events):
        self.sem, self.events, self.made = sem, list(events), 0
        self.value = {e: n + 1 for n, e in enumerate(self.events)}

    def mark(self, *event):
        assert self.events[self.made] == event, (self.events[self.made], event)
        self.made += 1
        return self.sem, 1

    def after(self, *event):
        return self.sem, self.value[event]


def weight_stream():
    def ada(pc):
        return [("ada", 2 * pc + n, kh) for n in range(2) for kh in range(2)]

    u = ada(0) + ada(1)
    u += [("in", n, kh) for n in range(4) for kh in range(2)] + [("poolw",)]
    for j in range(PAIRS):
        u += [("in", 4 + j, kh) for kh in range(2)]
        u += ada(2 + j)
    u += [("ba", 0), ("bp", 0), ("ba", 1), ("bp", 1)]
    u += [("out", n, kh) for n in range(2) for kh in range(2)]
    for j in range(FB0 // 2):
        u += [("up", 0, j), ("up", 1, j)]
    u += [("down", t) for t in range(FB0 // 2)]
    for l in (0, 1):
        u += [("in2", l, n, kh) for n in range(3) for kh in range(2)]
        u += [("ucb", l, w, h) for w in range(3) for h in range(2)]
        u += [("pproj", l)]
        u += [("wo", l, n, kh) for kh in (1, 0) for n in range(2)]
        if l == 0:
            for n in range(NF):
                u += [("d1", n, kh) for kh in range(2)] + [("d3", n, kh) for kh in range(2)]
            u += [("d2", t) for t in range(KF // 2)]
            u += [("pgate", n, kh) for n in range(2) for kh in range(2)]
    return u


DIRECT = ("poolw", "ba", "bp", "pproj")


def fused_blocks(nc, a, out):
    with ExitStack() as ctx:
        def sb(name, shape, dt=F32):
            return ctx.enter_context(nc.sbuf_tensor(name, shape, dt))

        def sem(name):
            return ctx.enter_context(nc.semaphore(name))

        raw = sb("raw", [P, RAW, UNIT])
        whi, wlo = sb("whi", [P, HALF, UNIT], F32R), sb("wlo", [P, HALF, UNIT], F32R)
        h = sb("h", [P, TT, D])
        xn = sb("xn", [P, TT, D])
        ah, al = sb("ah", [P, KD, S], F32R), sb("al", [P, KD, S], F32R)
        consts = sb("consts", [P, C_END])
        vec = sb("vec", [P, NVT * P])
        pinT = sb("pinT", [P, 2, DPLE // P, S])
        work_at = -(-nc.sbuf_base // 32) * 32
        work = sb("work", [P, ARENA])
        gh = nc.alloc_sbuf_tensor_at("gh", [P, KF, S], F32R, offset=work_at)
        gl = nc.alloc_sbuf_tensor_at("gl", [P, KF, S], F32R, offset=work_at + 4 * KF * S)
        stat = sb("stat", [P, 256])
        modc = sb("modc", [P, 48])
        acol = sb("acol", [P, 2, KD])
        cact = sb("cact", [P, KD])
        cparts = sb("cparts", [P, KD, 2], F32R)
        router = sb("router", [P, KD, EXPERTS])
        rh, rl = sb("rh", [P, KD, EXPERTS], F32R), sb("rl", [P, KD, EXPERTS], F32R)
        ones = sb("ones", [P, P])
        epsc = sb("epsc", [P, 1])
        flag = sb("flag", [P, 1], I32)
        slot_of = sb("slot_of", [P, TT, 2 * EXPERTS + 1])
        rel_dram = nc.dram_tensor("bias_by_distance", [HEADS, RELV], F32).ap()

        def wk(lo, *shape):
            n = int(np.prod(shape))
            v = work[:, lo:lo + n]
            if len(shape) == 2:
                return v.rearrange("p (a b) -> p a b", a=shape[0])
            if len(shape) == 3:
                return v.rearrange("p (a b c) -> p a b c", a=shape[0], b=shape[1])
            return v

        qkn = wk(0, 2, TT, AW)
        poolT, poolF = wk(0, CA, S), wk(1024, CA, S)
        qkT = wk(2048, 2, PAIRS, S)
        v = wk(4096, TT, AW)
        pin = wk(5120, TT, GROUPS * P)
        uF = wk(5120, CA, S)
        sc = wk(6144, 2, 2, TRI)
        pr = wk(7680, 2, 2, TRI)
        pT = wk(9216, 2, 2, TRI)
        attnT = wk(10752, CA, S)
        sq = wk(11776, 2, AW)
        biasT = wk(12800, HEADS, TRI)
        cuF, convF, sqF = wk(12800, CA, S), wk(13824, CA, S), wk(14848, CA, S)
        gate_row = wk(12800, D)
        gate_a = wk(15872, TT, D)
        mod_row = wk(17920, D)[0:2]
        pp = wk(ARENA - TT * D, TT, D)
        vrow = wk(0, NVT, P)
        psrc = wk(1024, 2, TT, DPLE)
        relsel = wk(2048, RELV)
        relw = wk(2560, HEADS)
        relv = wk(2600, RELV)
        relrev = wk(9216, HEADS, S)
        modulated = wk(0, KD, S)
        AFTER = 2 * KF * S
        g_tmp = wk(AFTER, 4, 512)
        g_mul = wk(AFTER + 2048, 2, 512)
        cv = wk(AFTER, 4, 2, S)
        prod = wk(AFTER + 2048, 2, S)
        sA = wk(3584, 2, 512)
        hm = wk(4608, 2, 512)
        yg = wk(5632, D)
        pick = wk(6656, TT, P)
        pshare = wk(6912, TT, P)
        LATE = KF * S + KF * P
        shareT = wk(LATE, TT, P)
        choice = wk(LATE + 256, 8, TT * EXPERTS).rearrange("p k (t e) -> p k t e", t=TT)
        share_of = wk(LATE + 384, TT, 2 * EXPERTS + 1)
        xg = wk(LATE + 512, KD, P)
        psig = wk(3584, 4, 512)
        eh, el = gh[:, 0:KF // 2, :], gl[:, 0:KF // 2, :]
        eh, el = (x.rearrange("p c (a t) -> p (c a) t", a=2) for x in (eh, el))
        xh, xl = ah[:, :, 0:P], al[:, :, 0:P]
        ident = consts[:, C_ID:C_ID + P]
        anti = consts[:, C_ANTI:C_ANTI + P]
        ge = consts[:, C_GE:C_GE + P]
        before = consts[:, C_LT:C_LT + P]
        iota = consts[:, C_IOTA:C_IOTA + P]
        mask = consts[:, C_MASK:C_MASK + TRI]
        band = consts[:, C_BAND:C_RANK].rearrange("p (g n) -> p g n", g=GROUPS)
        rank = consts[:, C_RANK:C_END]

        def col(name, i):
            return vec[:, VROWS[name][0] + i:VROWS[name][0] + i + 1]

        def cols(name, i, n):
            return vec[:, VROWS[name][0] + i:VROWS[name][0] + i + n]

        main = [ctx.enter_context(nc.psum_tensor(f"main{i}", [P, 512], F32)) for i in range(4)]
        wide = [ctx.enter_context(nc.psum_tensor(n, [P, 1024], F32)) for n in ("X", "Y")]
        bank = main + wide
        X, Y = 4, 5
        filled = [sem(f"filled_{n}") for n in ("m0", "m1", "m2", "m3", "X", "Y")]
        drained = [sem(f"drained_{n}") for n in ("m0", "m1", "m2", "m3", "X", "Y")]
        uses, where = [0] * 6, {}
        turn = [0]

        def bank_open(pe, key, b=None):
            if b is None:
                b = turn[0] % 4
                turn[0] += 1
            if uses[b]:
                pe.wait_ge(drained[b], uses[b])
            uses[b] += 1
            where[key] = [b, uses[b], None]
            return bank[b]

        def bank_full(ins, key):
            ins.then_inc(filled[where[key][0]], 1)
            n = min(taken[0] + 2, NS)
            while n and any(at_unit[u] <= split_at[n - 1] - RAW for u in list(direct_no)[reported[0]:]):
                n -= 1
            where[key][2] = n

        taken, reported, ahead = [0], [0], []

        def keep_ahead(eng, key):
            for e, split_to in ahead:
                if e is eng:
                    split_to(where[key][2])

        def result(eng, key):
            keep_ahead(eng, key)
            b, n, _ = where[key]
            eng.wait_ge(filled[b], n)
            return bank[b]

        def read_out(ins, key):
            ins.then_inc(drained[where[key][0]], 1)

        def moved(eng, *key):
            keep_ahead(eng, key)
            b, n, _ = where[key]
            eng.wait_ge(drained[b], n)

        NORMS = range(8)

        def signal(name, events):
            return Signal(sem(name), events)

        loaded = {k: sem(f"loaded_{k}") for k in ("consts", "x", "vrow", "rel", "relrev", "p", "router")}
        rel_stored = sem("rel_stored")
        raw_loaded = [sem(f"raw_loaded_{i}") for i in range(RAW)]
        hi_ready, lo_ready = sem("hi_ready"), sem("lo_ready")
        unit_used, direct_used = sem("unit_used"), sem("direct_used")
        turn_hi = sem("turn_hi")
        turn_his = Signal(turn_hi, HI_STEPS)
        small_set = sem("small_set")
        cact_hi, cact_lo = sem("cact_hi"), sem("cact_lo")
        acol_ready = signal("acol_ready", [(0,), (1,)])
        std_ready = signal("std_ready", [(m, tt) for m in NORMS for tt in range(TT)])
        xn_ready = signal("xn_ready", [(m, tt) for m in NORMS for tt in range(TT)])
        QK = [(l, w, tt) for l in range(3) for w in range(2) for tt in range(TT)]
        qk_sq = signal("qk_sq", QK)
        qk_sumsq = signal("qk_sumsq", QK)
        qk_std = signal("qk_std", QK)
        heads0 = [(j,) for j in range(PAIRS)]
        heads12 = [(l, j) for l in (1, 2) for j in range(PAIRS)]
        nmax_ready = signal("nmax_ready", heads0)
        exp_ready = signal("exp_ready", heads0)
        prob_ready = signal("prob_ready", heads0)
        ln_ready = signal("ln_ready", heads12)
        sp_ready = signal("sp_ready", heads12)
        weight_ready = signal("weight_ready", heads12)
        sig_ready = signal("sig_ready", [(0,), (1,)])
        merged_ready = signal("merged_ready", [(n, tt) for n in range(2) for tt in range(TT)])
        h_ready = signal("h_ready", [(m, tt) for m in (1, 2, 5, 7, 8) for tt in range(TT)])
        taps_ready = signal("taps_ready", [(j, half, b) for j in range(FB0 // 2) for half in range(2) for b in range(2)])
        cg_ready = signal("cg_ready", [(j,) for j in range(FB0 // 2)])
        gT_ready = signal("gT_ready", [(j,) for j in range(FB0 // 2)])
        MX = [(l, w) for l in (1, 2) for w in ("conv", "attn")]
        msq_ready = signal("msq_ready", MX)
        scaled_ready = signal("scaled_ready", MX)
        scaled_hi = signal("scaled_hi", MX)
        mixed_ready = signal("mixed_ready", MX)
        rsF = wk(11776, S)
        chosen_ready = sem("chosen_ready")
        margin_ready = sem("margin_ready")
        margin_exp = sem("margin_exp")
        flag_ready = sem("flag_ready")
        e_pick = sem("e_pick")
        e_filled = [sem(f"e_filled_{b}") for b in range(6)]
        e_drained = [sem(f"e_drained_{b}") for b in range(6)]
        e_rows, e_zeroed = sem("e_rows"), sem("e_zeroed")
        last_yg, last_share, last_rows = sem("last_yg"), sem("last_share"), sem("last_rows")
        e_hi, e_xg, e_xgh, e_xgl = sem("e_hi"), sem("e_xg"), sem("e_xgh"), sem("e_xgl")
        tail_loaded = [sem(f"tail_loaded_{i}") for i in range(4)]
        tail_hi, tail_lo, tail_used = sem("tail_hi"), sem("tail_lo"), sem("tail_used")
        router_hi, router_lo = sem("router_hi"), sem("router_lo")
        g_prod = signal("g_prod", [(j,) for j in range(FB0 // 2)])
        stored = sem("stored")
        dve_step = sem("dve_step")
        act_step = sem("act_step")

        E_USES = {0: 4, 1: 4, 2: 4, 3: 4, X: 6, Y: 5}

        def e_at(name, n=0):
            if name in ("up", "gate"):
                b = (2 * n + (name == "up")) % 4
                return b, n // 2
            return {"rows": (Y if n else X, 0), "share": (X, 1), "y": (2 + n, 3), "gather": (X, 5),
                    "turn": (X, 2 + n // 2) if n % 2 else (Y, 1 + n // 2)}[name]

        def e_count(i, name, n=0):
            b, k = e_at(name, n)
            return b, i * E_USES[b] + (k + 2)

        units = weight_stream()
        at_unit = {u: n for n, u in enumerate(units)}
        split_no, direct_no = {}, {}
        for u in units:
            own = direct_no if u[0] in DIRECT else split_no
            own[u] = len(own)
        split_at = [at_unit[u] for u in split_no]
        NU, NS = len(units), len(split_no)
        assert 2 * UE % RAW == 0 and 2 * UE % HALF == 0 and all(u in split_no for u in units[-RAW:])

        def kn(w, kh, n):
            return w[kh * 512:(kh + 1) * 512, n * 512:(n + 1) * 512].rearrange("(k p) n -> p k n", p=P)

        def k8(w, c0):
            return w[:, c0:c0 + 256].rearrange("(k p) n -> p k n", p=P)

        def k2(w, t):
            return w[t * 256:(t + 1) * 256, :].rearrange("(k p) n -> p k n", p=P)

        def source(u):
            k = u[0]
            if k == "ada":
                return kn(a["ada_w"][0], u[2], u[1])
            if k == "in":
                return kn(a["w_in"][0], u[2], u[1])
            if k == "poolw":
                return a["pool_w"][0].rearrange("g c d -> c g d")
            if k in ("ba", "bp"):
                return kn(a["w_branch_attn" if k == "ba" else "w_branch_pool"][0], 0, u[1])
            if k == "out":
                return kn(a["w_out"][0], u[2], u[1])
            if k == "up":
                return k8(a["w_up"][0], u[1] * FF0 + u[2] * 256)
            if k == "down":
                return k2(a["w_down"][0], u[1])
            if k == "in2":
                return kn(a["w_in_2"][u[1]], u[3], u[2])
            if k == "ucb":
                return k8(a["w_in_2"][u[1]], 3 * AW + u[2] * 512 + u[3] * 256)
            if k == "pproj":
                return k2(a["ple_proj_w_2"][u[1]], 0)
            if k == "wo":
                return kn(a["w_o_2"][u[1]], u[3], u[2])
            if k == "d1":
                return kn(a["dense_w1_2"][0], u[2], u[1])
            if k == "d3":
                return kn(a["dense_w3_2"][0], u[2], u[1])
            if k == "d2":
                return k2(a["dense_w2_2"][0], u[1])
            return kn(a["ple_gate_w_2"][0], u[2], u[1])

        def slot(n, kc, width):
            return raw[:, n % RAW, 0:kc * width].rearrange("p (k n) -> p k n", k=kc)

        def parts(s, kc, width):
            return [x[:, s % HALF, 0:kc * width].rearrange("p (k n) -> p k n", k=kc) for x in (whi, wlo)]

        block = ctx.enter_context(nc.Block())

        @block.tensor
        def _(pe):
            tr = nc.tensor.transpose
            owed = {"unit": 0, "direct": 0}
            keep = [0]

            def mm(out, lhsT, rhs, start, stop):
                ins = nc.tensor.matmul(out, lhsT, rhs, start=start, stop=stop)
                if not stop and owed["unit"] > keep[0]:
                    ins.then_inc(unit_used, owed["unit"] - keep[0])
                    owed["unit"] = keep[0]
                elif not stop and owed["direct"]:
                    ins.then_inc(direct_used, owed["direct"])
                    reported[0] += owed["direct"]
                    owed["direct"] = 0
                return ins

            def mm3(out, lhsT, rhs, start, stop):
                mm(out, lhsT[1], rhs[0], start, False)
                mm(out, lhsT[0], rhs[1], False, False)
                return mm(out, lhsT[0], rhs[0], False, stop)

            def cut(x, *at):
                return x[0][at], x[1][at]

            a_parts, g_parts = (ah, al), (gh, gl)

            def free_units(n=1):
                owed["unit"] += n

            def free_direct(n=1):
                owed["direct"] += n

            def direct(u, kc, width):
                n = at_unit[u]
                pe.wait_ge(raw_loaded[n % RAW], 16 * (n // RAW + 1))
                return slot(n, kc, width)

            def unit(u, kc, width):
                s = split_no[u]
                assert s == taken[0]
                taken[0] += 1
                pe.wait_ge(lo_ready, s + 1)
                return parts(s, kc, width)

            def norm_turn(m, src=xn):
                for q, b in ((0, X), (1, Y)):
                    o = bank_open(pe, ("norm", m, q), b)
                    o = o[:, :].rearrange("p (c t) -> p c t", t=S)
                    for tt in range(TT):
                        if q == 0:
                            pe.wait_ge(*xn_ready.after(m, tt))
                        for c in range(4):
                            last = tr(o[:, c, tt * P:(tt + 1) * P], src[:, tt, (4 * q + c) * P:(4 * q + c + 1) * P], ident)
                    bank_full(last, ("norm", m, q))

            def wait_aT(kind, m):
                moved(pe, kind, m, 0)
                moved(pe, kind, m, 1)

            def project(name, key, fresh=None, get=unit, done=free_units):
                outs = [bank_open(pe, (*key, tt)) for tt in range(TT)]
                for kh in range(2):
                    w = get((*name, kh), 4, 512)
                    if fresh:
                        moved(pe, *fresh, kh)
                    for tt in range(TT):
                        for k in range(4):
                            kk = 4 * kh + k
                            last = mm3(outs[tt][:, :], cut(a_parts, slice(None), kk, slice(tt * P, (tt + 1) * P)),
                                       cut(w, slice(None), k), kk == 0, kk == KD - 1)
                        if kh == 1:
                            bank_full(last, (*key, tt))
                    done()

            def feature_block(w, b, o):
                for k in range(KD):
                    last = mm3(o[:, 0:S], cut(w, slice(None), k, slice(b * P, (b + 1) * P)), cut(a_parts, slice(None), k),
                               k == 0, k == KD - 1)
                return last

            def gemv(pc):
                for n in range(2):
                    o = bank_open(pe, ("modrow", pc, n))
                    for kh in range(2):
                        w = unit(("ada", 2 * pc + n, kh), 4, 512)
                        for k in range(4):
                            kk = 4 * kh + k
                            mm(o[0:2, :], cparts[:, kk, :], w[1][:, k, :], kk == 0, False)
                            last = mm(o[0:2, :], cparts[:, kk, :], w[0][:, k, :], False, kk == KD - 1)
                        if kh == 1:
                            bank_full(last, ("modrow", pc, n))
                        free_units()

            def mod_turn(pc):
                o = bank_open(pe, ("mod", pc))
                for c in range(KD):
                    if c % 4 == 0:
                        moved(pe, "modrow", pc, c // 4)
                    last = mm(o[:, c:c + 1], mod_row[:, c * P:(c + 1) * P], ones[0:2, 0:1], start=True, stop=True)
                bank_full(last, ("mod", pc))

            def gate_rows(g):
                moved(pe, "mod", 2 + 3 * g)
                for n in range(2):
                    o = bank_open(pe, ("grow", g, n))
                    for c in range(4):
                        s = modc[:, (2 + 3 * g) * KD + 4 * n + c:(2 + 3 * g) * KD + 4 * n + c + 1]
                        last = mm(o[:, c * P:(c + 1) * P], s.broadcast_to([P, P]), ident, start=True, stop=True)
                    bank_full(last, ("grow", g, n))

            def qk_turn(l, w):
                o = bank_open(pe, ("qkT", l, w), X if w == 0 else Y)
                o = o[:, :].rearrange("p (j t) -> p j t", t=S)
                for tt in range(TT):
                    moved(pe, "qk"[w], l, tt)
                    for j in range(PAIRS):
                        last = tr(o[:, j, tt * P:(tt + 1) * P], qkn[:, w, tt, j * P:(j + 1) * P], ident)
                bank_full(last, ("qkT", l, w))

            def head(x, j, e):
                return x[DH * e:DH * (e + 1), j, :]

            def scores(l, j):
                if j == 0:
                    moved(pe, "qkT", l, 0)
                    moved(pe, "qkT", l, 1)
                o = bank_open(pe, ("score", l, j), X)
                for e in range(2):
                    q, k = head(qkT[:, 0], j, e), head(qkT[:, 1], j, e)
                    at = 512 * e
                    if l == 0:
                        mm(o[:, at:at + S], q[:, P:S], k[:, :], start=True, stop=True)
                        last = mm(o[:, at + S:at + TRI], q[:, 0:P], k[:, 0:P], start=True, stop=True)
                    else:
                        mm(o[:, at:at + S], k[:, 0:P], q[:, :], start=True, stop=True)
                        last = mm(o[:, at + S:at + TRI], k[:, P:S], q[:, P:S], start=True, stop=True)
                bank_full(last, ("score", l, j))

            def prob_turn(j):
                pe.wait_ge(*prob_ready.after(j))
                o = bank_open(pe, ("probT", j), Y)
                for e in range(2):
                    s = pr[:, j % 2, e, :]
                    at = 512 * e
                    tr(o[:, at:at + P], s[:, S:TRI], ident)
                    tr(o[:, at + P:at + S], s[:, 0:P], ident)
                    last = tr(o[:, at + S:at + TRI], s[:, P:S], ident)
                bank_full(last, ("probT", j))

            def later_sums(l, j):
                pe.wait_ge(*sp_ready.after(l, j))
                o = bank_open(pe, ("later", l, j), Y)
                for e in range(2):
                    s = pr[:, j % 2, e, :]
                    at = 512 * e
                    mm(o[:, at + S:at + TRI], ge, s[:, S:TRI], start=True, stop=True)
                    mm(o[:, at:at + S], ge, s[:, 0:S], start=True, stop=False)
                    last = mm(o[:, at + P:at + S], ones[:, :], s[:, S:TRI], start=False, stop=True)
                bank_full(last, ("later", l, j))

            def values(l, j):
                if l == 0:
                    moved(pe, "probT", j)
                else:
                    pe.wait_ge(*weight_ready.after(l, j))
                if j == 0:
                    moved(pe, "v", l, 0)
                    moved(pe, "v", l, 1)
                o = bank_open(pe, ("attn", l, j))
                for e in range(2):
                    hd = 2 * j + e
                    w = pT[:, j % 2, e, :]
                    mm(o[DH * e:DH * (e + 1), 0:S], v[:, 0, hd * DH:(hd + 1) * DH], w[:, 0:S],
                       start=True, stop=False)
                    last = mm(o[DH * e:DH * (e + 1), P:S], v[:, 1, hd * DH:(hd + 1) * DH], w[:, S:TRI],
                              start=False, stop=True)
                bank_full(last, ("attn", l, j))

            def out_rows(name, key, fresh):
                for n in range(2):
                    project((*name, n), (*key, n), fresh if n == 0 else None)

            def down_rows(name, key, count):
                outs = [[bank_open(pe, (*key, n, tt)) for n in range(2)] for tt in range(TT)]
                for t in range(count):
                    w = unit((*name, t), 2, D)
                    down_wait(name, t)
                    for tt in range(TT):
                        for n in range(2):
                            for k in range(2):
                                kk = 2 * t + k
                                last = mm3(outs[tt][n][:, :], cut(g_parts, slice(None), kk, slice(tt * P, (tt + 1) * P)),
                                           cut(w, slice(None), k, slice(n * 512, (n + 1) * 512)), kk == 0, kk == 2 * count - 1)
                            if t == count - 1:
                                bank_full(last, (*key, n, tt))
                    free_units()

            def down_wait(name, t):
                if name == ("down",):
                    pe.wait_ge(*gT_ready.after(t))
                elif t % 2 == 0:
                    moved(pe, "gT", t // 2)

            pe.wait_ge(loaded["consts"], 16)
            pe.wait_ge(loaded["vrow"], 16)
            o = bank_open(pe, ("vec",), X)
            for t in range(NVT):
                last = tr(o[:, t * P:(t + 1) * P], vrow[:, t, :], ident)
            bank_full(last, ("vec",))
            norm_turn(0)
            pe.wait_ge(loaded["rel"], 32)
            pe.wait_ge(small_set, 3)
            o = bank_open(pe, ("relv",))
            bank_full(mm(o[0:HEADS, :], relw[0:BUCKETS + 1, :], relsel[0:BUCKETS + 1, :], start=True, stop=True), ("relv",))
            pe.wait_ge(loaded["p"], 32)
            for l in range(2):
                o = bank_open(pe, ("pinT", l))
                for k in range(DPLE // P):
                    for tt in range(TT):
                        last = tr(o[:, k * S + tt * P:k * S + (tt + 1) * P], psrc[:, l, tt, k * P:(k + 1) * P], ident)
                bank_full(last, ("pinT", l))
            pe.wait_ge(cact_lo, 1)
            gemv(0)
            mod_turn(0)
            gemv(1)
            mod_turn(1)
            pe.wait_ge(loaded["relrev"], 16)
            for n in range(4):
                o = bank_open(pe, ("bias", n))
                bank_full(mm(o[:, :], anti, relrev[:, 2 * n:2 * n + 2, :], start=True, stop=True), ("bias", n))

            project(("in", 0), ("q", 0), ("norm", 0))
            project(("in", 1), ("k", 0))
            qk_turn(0, 0)
            project(("in", 2), ("v", 0))
            qk_turn(0, 1)
            project(("in", 3), ("p", 0))
            scores(0, 0)
            for tt in range(TT):
                moved(pe, "p", 0, tt)
            o = bank_open(pe, ("poolT",), Y)
            for g in range(GROUPS):
                mm(o[:, g * S:(g + 1) * S], pin[:, 0, g * P:(g + 1) * P], band[:, g, 0:S], start=True, stop=False)
                last = mm(o[:, g * S + P:(g + 1) * S], pin[:, 1, g * P:(g + 1) * P], band[:, g, S:TRI],
                          start=False, stop=True)
            bank_full(last, ("poolT",))
            for j in range(PAIRS):
                if j == 0:
                    pw = direct(("poolw",), 4, P)
                    moved(pe, "poolT")
                    for g in range(GROUPS):
                        if g % 2 == 0:
                            o = bank_open(pe, ("poolF", g // 2))
                        last = mm(o[:, (g % 2) * S:(g % 2 + 1) * S], pw[:, g, :], poolT[:, g, :], start=True, stop=True)
                        if g % 2:
                            bank_full(last, ("poolF", g // 2))
                    free_direct()
                project(("in", 4 + j), ("gate", j))
                gemv(2 + j)
                prob_turn(j)
                if j < PAIRS - 1:
                    scores(0, j + 1)
                mod_turn(2 + j)
                values(0, j)
            gate_rows(0)
            for j in range(PAIRS):
                moved(pe, "attn", 0, j)
            moved(pe, "poolF", 0)
            moved(pe, "poolF", 1)
            for n in range(2):
                wa, wp = direct(("ba", n), 4, 512), direct(("bp", n), 4, 512)
                for tt in range(TT):
                    for nm, w, s in (("ba", wa, attnT), ("bp", wp, poolF)):
                        o = bank_open(pe, (nm, n, tt))
                        for k in range(CA):
                            last = mm(o[:, :], s[:, k, tt * P:(tt + 1) * P], w[:, k, :],
                                      start=(k == 0), stop=(k == CA - 1))
                        bank_full(last, (nm, n, tt))
                free_direct(2)
            for q, b in ((0, X), (1, Y)):
                o = bank_open(pe, ("merged", 0, q), b)
                o = o[:, :].rearrange("p (c t) -> p c t", t=S)
                for tt in range(TT):
                    pe.wait_ge(*merged_ready.after(q, tt))
                    for c in range(4):
                        last = tr(o[:, c, tt * P:(tt + 1) * P], gate_a[:, tt, (4 * q + c) * P:(4 * q + c + 1) * P], ident)
                bank_full(last, ("merged", 0, q))
            out_rows(("out",), ("out", 0), ("merged", 0))
            gate_rows(1)
            norm_turn(1)
            wait_aT("norm", 1)
            for j in range(FB0 // 2):
                for half in range(2):
                    w = unit(("up", half, j), 8, 256)
                    for b in range(2):
                        o = bank_open(pe, ("up", j, half, b))
                        bank_full(feature_block(w, b, o), ("up", j, half, b))
                    free_units()
            down_rows(("down",), ("down", 0), FB0 // 2)

            for l in (1, 2):
                li = l - 1
                m0 = 2 + 3 * li
                norm_turn(m0)
                project(("in2", li, 0), ("q", l), ("norm", m0))
                project(("in2", li, 1), ("k", l))
                qk_turn(l, 0)
                project(("in2", li, 2), ("v", l))
                qk_turn(l, 1)

                half = [None, None]

                def ucb(n):
                    if n % 2 == 0:
                        half[:] = unit(("ucb", li, n // 4, (n % 4) // 2), 8, 256)
                    o = bank_open(pe, ("ucb", l, n))
                    bank_full(feature_block(half, n % 2, o), ("ucb", l, n))
                    if n % 2:
                        free_units()

                def pproj(w, n):
                    for tt in range(TT):
                        o = bank_open(pe, ("pproj", l, n, tt))
                        for k in range(2):
                            last = mm(o[:, :], pinT[:, li, k, tt * P:(tt + 1) * P], w[:, k, n * 512:(n + 1) * 512],
                                      start=(k == 0), stop=(k == 1))
                        bank_full(last, ("pproj", l, n, tt))

                def mean(which, b):
                    pe.wait_ge(*msq_ready.after(l, which))
                    o = bank_open(pe, ("mean", l, which), b)
                    for c in range(CA):
                        last = mm(o[:, 0:S], ones[:, :], sqF[:, c, :], start=(c == 0), stop=(c == CA - 1))
                    bank_full(last, ("mean", l, which))

                def wo_half(outs, n, kh):
                    w = unit(("wo", li, n, kh), 4, 512)
                    pe.wait_ge(*mixed_ready.after(l, ("attn", "conv")[kh]))
                    for tt in range(TT):
                        for k in range(4):
                            kk = 4 * kh + k
                            last = mm3(outs[tt][:, :], cut(a_parts, slice(None), kk, slice(tt * P, (tt + 1) * P)),
                                       cut(w, slice(None), k), kk == 4, kk == 3)
                        if kh == 0:
                            bank_full(last, ("wo", l, n, tt))
                    free_units()

                ucb(0)
                scores(l, 0)
                for n in (1, 2, 3):
                    ucb(n)
                for j in range(PAIRS):
                    later_sums(l, j)
                    if j < PAIRS - 1:
                        scores(l, j + 1)
                    if j < PAIRS - 1:
                        for n in ((4, 5, 6), (7, 8, 9), (10, 11))[j]:
                            ucb(n)
                    else:
                        w = direct(("pproj", li), 2, D)
                        pproj(w, 0)
                        mean("conv", X)
                        pproj(w, 1)
                        free_direct()
                    values(l, j)
                outs = []
                for n in range(2):
                    outs.append([bank_open(pe, ("wo", l, n, tt)) for tt in range(TT)])
                    wo_half(outs[n], n, 1)
                    if n == 0:
                        mean("attn", Y)
                for n in range(2):
                    wo_half(outs[n], n, 0)
                norm_turn(m0 + 1)
                if l == 1:
                    def hidden_turn(n):
                        o = bank_open(pe, ("gT", n), (X, Y)[n % 2])
                        o = o[:, :].rearrange("p (c t) -> p c t", t=S)
                        for tt in range(TT):
                            moved(pe, "d3", n, tt)
                            for c in range(4):
                                last = tr(o[:, c, tt * P:(tt + 1) * P], g_mul[:, tt, c * P:(c + 1) * P], ident)
                        bank_full(last, ("gT", n))

                    for n in range(NF):
                        project(("d1", n), ("d1", n), ("norm", m0 + 1) if n == 0 else None)
                        if n:
                            hidden_turn(n - 1)
                        project(("d3", n), ("d3", n))
                    hidden_turn(NF - 1)
                    down_rows(("d2",), ("d2", 0), KF // 2)
                    norm_turn(m0 + 2)
                    out_rows(("pgate",), ("pgate", l), ("norm", m0 + 2))

            wait_aT("norm", 6)
            keep[0] = 1
            pe.wait_ge(router_lo, 1)
            o = bank_open(pe, ("logits",))
            for tt in range(TT):
                for k in range(KD):
                    x, w = cut(a_parts, slice(None), k, slice(tt * P, (tt + 1) * P)), (rh[:, k, :], rl[:, k, :])
                    for n, (xi, wi) in enumerate(((1, 1), (1, 0), (0, 1), (0, 0))):
                        last = mm(o[:, tt * EXPERTS:(tt + 1) * EXPERTS], x[xi], w[wi],
                                  start=(k + n == 0), stop=(k == KD - 1 and n == 3))
            bank_full(last, ("logits",))
            pe.wait_ge(chosen_ready, 1)
            chosen = choice[:, 6]
            o = bank_open(pe, ("slots",))
            mm(o[:, 0:8], before, chosen[:, 0, :], start=True, stop=True)
            mm(o[:, 8:16], ones[:, :], chosen[:, 0, :], start=True, stop=False)
            mm(o[:, 8:16], before, chosen[:, 1, :], start=False, stop=True)
            mm(o[:, 16:24], ones[:, :], chosen[:, 0, :], start=True, stop=False)
            bank_full(mm(o[:, 16:24], ones[:, :], chosen[:, 1, :], start=False, stop=True), ("slots",))
            for b in range(6):
                pe.wait_ge(drained[b], uses[b])
            for b in (0, 1, 2, 3, Y):
                pe.sem_inc(e_drained[b], 1)
                pe.sem_inc(e_filled[b], 1)

            def gather():
                for c in range(KD):
                    for tt in range(TT):
                        last = mm(wide[0][:, c * P:(c + 1) * P], xn[:, tt, c * P:(c + 1) * P], pick[:, tt, :],
                                  start=(tt == 0), stop=(tt == TT - 1))
                last.then_inc(e_filled[X], 1)

            def scatter(tt):
                for n in range(2):
                    last = mm(wide[tt][:, n * 512:(n + 1) * 512], shareT[:, tt, :], yg[:, n * 512:(n + 1) * 512],
                              start=True, stop=True)
                return last

            def expert(it, odd):
                i = it * 2 + odd

                def take(name, n=0):
                    b, count = e_count(i, name, n)
                    pe.wait_ge(e_drained[b], count - 1)
                    return bank[b]

                def full(ins, name, n=0):
                    ins.then_inc(e_filled[e_at(name, n)[0]], 1)

                def eunit(s, kc, width):
                    n = NS + odd * UE + s
                    pe.wait_ge(lo_ready, it * (2 * UE) + (n + 1))
                    return parts(n, kc, width)

                def hidden(s, name, n):
                    o = take(name, n)
                    for kh in range(2):
                        w = eunit(s + kh, 4, 512)
                        for k in range(4):
                            kk = 4 * kh + k
                            last = mm3(o[:, :], (xh[:, kk, :], xl[:, kk, :]), cut(w, slice(None), k), kk == 0, kk == KD - 1)
                        free_units()
                    full(last, name, n)

                def turn(n):
                    b, count = e_count(i, "up", n)
                    pe.wait_ge(e_drained[b], count)
                    o = take("turn", n)
                    for c in range(4):
                        last = tr(o[:, c * P:(c + 1) * P], hm[:, n % 2, c * P:(c + 1) * P], ident)
                    full(last, "turn", n)

                pe.wait_ge(e_xgl, i + 1)
                for n in range(NF):
                    hidden(4 * n, "gate", n)
                    if n == 0:
                        pe.wait_ge(e_drained[2], i * E_USES[2] + 1)
                        pe.wait_ge(e_drained[3], i * E_USES[3] + 1)
                        for tt in range(TT):
                            take("rows", tt)
                            full(scatter(tt), "rows", tt)
                        o = take("share")
                        for tt in range(TT):
                            last = tr(o[:, tt * P:(tt + 1) * P], pshare[:, tt, :], ident)
                        full(last, "share")
                    else:
                        turn(n - 1)
                    hidden(4 * n + 2, "up", n)
                ys = [take("y", 0), take("y", 1)]
                for t in range(KF // 2):
                    w = eunit(4 * NF + t, 2, D)
                    if t % 2 == 0:
                        b, count = e_count(i, "turn", t // 2)
                        pe.wait_ge(e_drained[b], count)
                    for n in range(2):
                        for k in range(2):
                            last = mm3(ys[n][:, :], (eh[:, 2 * t + k, :], el[:, 2 * t + k, :]),
                                       cut(w, slice(None), k, slice(n * 512, (n + 1) * 512)),
                                       t + k == 0, t == KF // 2 - 1 and k == 1)
                        if t == KF // 2 - 1:
                            full(last, "y", n)
                    free_units()
                    if t == 1:
                        turn(NF - 1)
                    if t == 5:
                        pe.wait_ge(e_pick, i + 2)
                        take("gather")
                        gather()

            def passes(first):
                owed["unit"], keep[0] = 1, 0
                with pe.Fori(first // 2, first // 2 + EXPERTS // 2) as it:
                    for odd in range(2):
                        expert(it, odd)
                assert owed == {"unit": 1, "direct": 0}

            pe.wait_ge(e_zeroed, 1)
            pe.wait_ge(e_pick, 1)
            gather()
            assert owed == {"unit": 1, "direct": 0}
            passes(0)
            pe.wait_ge(flag_ready, 1)
            over = pe.value_load(flag[0:1, 0:1], min_val=0, max_val=1)
            with pe.If(over == 1):
                passes(EXPERTS)
            pe.wait_ge(last_yg, 1)
            pe.wait_ge(last_share, 1)
            for tt in range(TT):
                scatter(tt).then_inc(last_rows, 1)
            owed["unit"] = 0
            tail = [0]

            def tail_unit(u, kc, width):
                tail[0] += 1
                pe.wait_ge(tail_lo, tail[0])
                return parts(tail[0] - 1, kc, width)

            norm_turn(7)
            for n in range(2):
                outs = [bank_open(pe, ("pgate", 2, n, tt)) for tt in range(TT)]
                for kh in range(2):
                    w = tail_unit(None, 4, 512)
                    if n == 0:
                        moved(pe, "norm", 7, kh)
                    for tt in range(TT):
                        for k in range(4):
                            kk = 4 * kh + k
                            last = mm3(outs[tt][:, :], cut(a_parts, slice(None), kk, slice(tt * P, (tt + 1) * P)),
                                       cut(w, slice(None), k), kk == 0, kk == KD - 1)
                        if kh == 1:
                            bank_full(last, ("pgate", 2, n, tt))
                    if n + kh == 0:
                        last.then_inc(tail_used, 1)

        @block.sync
        def _(sp):
            sp.dma_start(consts[:, :], a["shape_consts"]).then_inc(loaded["consts"], 16)
            for n, u in enumerate(units):
                if n >= RAW:
                    old = units[n - RAW]
                    if old in split_no:
                        sp.wait_ge(lo_ready, split_no[old] + 1)
                    else:
                        sp.wait_ge(direct_used, direct_no[old] + 1)
                src = source(u)
                sp.dma_start(slot(n, src.shape[1], src.shape[2]), src).then_inc(raw_loaded[n % RAW], 16)

            def expert_unit(e, s):
                if s < 4 * NF:
                    w = a["moe_w1_2" if s % 4 < 2 else "moe_w3_2"][0]
                    src = w[e, (s % 2) * 512:(s % 2 + 1) * 512, (s // 4) * 512:(s // 4 + 1) * 512]
                else:
                    t = s - 4 * NF
                    src = a["moe_w2_2"][0][e, t * 256:(t + 1) * 256, :]
                return src.rearrange("(k p) n -> p k n", p=P)

            for s in range(2):
                n = NU + s
                sp.wait_ge(lo_ready, split_no[units[n - RAW]] + 1)
                sp.dma_start(slot(n, 4, 512), expert_unit(0, s)).then_inc(raw_loaded[n % RAW], 16)

            def passes(first):
                with sp.Fori(first // 2, (first + EXPERTS) // 2) as it:
                    for pos in range(2, 2 * UE + 2):
                        e = it * 2 + (pos // UE - first)
                        if pos >= 2 * UE:
                            e = (it * 2 + 2) % EXPERTS
                        n = NU + pos
                        sp.wait_ge(lo_ready, it * (2 * UE) + (NS + pos - RAW + 1))
                        src = expert_unit(e, pos % UE)
                        sp.dma_start(slot(n, src.shape[1], src.shape[2]), src).then_inc(raw_loaded[n % RAW], 16)
                sp.wait_ge(lo_ready, NS + (first + EXPERTS) * UE + 2)

            passes(0)
            sp.wait_ge(flag_ready, 1)
            over = sp.value_load(flag[0:1, 0:1], min_val=0, max_val=1)
            with sp.If(over == 1):
                passes(EXPERTS)
            for n in range(2):
                for kh in range(2):
                    sp.dma_start(slot(2 * n + kh, 4, 512), kn(a["ple_gate_w_2"][1], kh, n))\
                        .then_inc(tail_loaded[2 * n + kh], 16)
            for tt in range(TT):
                sp.wait_ge(*h_ready.after(8, tt))
                sp.dma_start(out[0, tt * P:(tt + 1) * P, :], h[:, tt, :]).then_inc(stored, 16)
            sp.wait_ge(stored, 32)

        @block.gpsimd
        def _(pool):
            pool.dma_start(relw[0:BUCKETS, :], a["rel_bias"]).then_inc(loaded["rel"], 16)
            pool.dma_start(relsel[0:BUCKETS + 1, :], a["shape_buckets"]).then_inc(loaded["rel"], 16)
            for l in range(2):
                pool.dma_start(psrc[:, l], a["p_2"][l, 0].rearrange("(t p) d -> p t d", p=P)).then_inc(loaded["p"], 16)
            pool.dma_start(router[:, :, :], a["router_w_2"][0].rearrange("(k p) e -> p k e", p=P)).then_inc(loaded["router"], 16)
            moved(pool, "relv")
            pool.dma_start(rel_dram, relv[0:HEADS]).then_inc(rel_stored, 16)
            pool.wait_ge(rel_stored, 16)
            rows = bass.AP(tensor=rel_dram.tensor, offset=rel_dram.offset, ap=[[1, P], [RELV, HEADS], [1, S]])
            pool.dma_start(relrev, rows).then_inc(loaded["relrev"], 16)

        def wait_h(eng, m, tt):
            if m in (3, 6):
                for n in range(2):
                    moved(eng, "wo", m // 3, n, tt)
            elif m == 4:
                for n in range(2):
                    moved(eng, "d2", 0, n, tt)
            else:
                if m in (1, 2):
                    keep_ahead(eng, (("out", "down")[m - 1], 0, 1, tt))
                eng.wait_ge(*h_ready.after(m, tt))

        def gain_of(m, c):
            return col(("mix_g", "ffn_g", "ple_g")[(m - 2) % 3], (m - 2) // 3 * KD + c)

        @block.scalar
        def _(act):
            fn = nc.scalar.activation
            steps = [0]
            split = [0]

            def split_to(n):
                for s in range(split[0], n):
                    at = split_at[s]
                    act.wait_ge(raw_loaded[at % RAW], 16 * (at // RAW + 1))
                    if s >= HALF:
                        act.wait_ge(unit_used, s - HALF + 1)
                    fn(whi[:, s % HALF, :], raw[:, at % RAW, :], ACT.Copy).then_inc(hi_ready, 1)
                split[0] = max(split[0], n)

            ahead.append((act, split_to))

            def then(ins):
                ins.then_inc(act_step, 1)
                steps[0] += 1
                act.wait_ge(act_step, steps[0])

            def rms_std(m):
                if m == 0:
                    act.wait_ge(small_set, 3)
                fn(stat[:, 200:201], epsc[:, 0:1], ACT.Sqrt)
                for tt in range(TT):
                    if m == 0:
                        act.wait_ge(loaded["x"], 16)
                    else:
                        wait_h(act, m, tt)
                    at = 4 * m + 2 * tt
                    then(fn(xn[:, tt, :], h[:, tt, :], ACT.Square, accum_out=stat[:, at:at + 1]))
                    fn(stat[:, at + 1:at + 2], stat[:, at:at + 1], ACT.Sqrt, bias=epsc[:, 0:1],
                       scale=1.0 / D).then_inc(*std_ready.mark(m, tt))

            def norm_out(m):
                for q in range(4):
                    if q % 2 == 0:
                        o = result(act, ("norm", m, q // 2))
                    for c in (2 * q, 2 * q + 1):
                        src = o[:, (c % 4) * S:(c % 4 + 1) * S]
                        if m < 2:
                            last = fn(modulated[:, c, :], src, ACT.Identity, bias=modc[:, 3 * m * KD + c:3 * m * KD + c + 1],
                                      scale=acol[:, m, c:c + 1])
                        else:
                            last = fn(ah[:, c, :], src, ACT.Copy, scale=gain_of(m, c))
                    last.then_inc(*turn_his.mark("norm", m, q))

            def qk_stats(l):
                for w in range(2):
                    for tt in range(TT):
                        o = result(act, ("qk"[w], l, tt))
                        fn(sq[:, tt, :], o[:, :], ACT.Square).then_inc(*qk_sq.mark(l, w, tt))
                        act.wait_ge(*qk_sumsq.after(l, w, tt))
                        at = 64 + 16 * (2 * w + tt)
                        fn(stat[:, at + 8:at + 16], stat[:, at:at + 8], ACT.Sqrt, bias=epsc[:, 0:1],
                           scale=1.0 / DH).then_inc(*qk_std.mark(l, w, tt))

            def copy_out(key, dst, n=512, func=ACT.Copy):
                o = result(act, key)
                read_out(fn(dst, o[:, 0:n], func), key)

            def turned(key, dst, step):
                o = result(act, key)
                fn(dst, o[:, (step % 2) * 512:(step % 2 + 1) * 512].rearrange("p (c t) -> p c t", t=S), ACT.Copy)\
                    .then_inc(*turn_his.mark(*key[:-1], step))

            act.dma_start(h[:, :, :], a["x"][0].rearrange("(t p) d -> p t d", p=P)).then_inc(loaded["x"], 16)
            act.dma_start(vrow, a["vector_rows"].rearrange("(t p) n -> p t n", p=P)).then_inc(loaded["vrow"], 16)
            rms_std(0)
            moved(act, "vec")
            then(fn(cact[:, :], cols("c", 0, KD), ACT.Silu))
            fn(cparts[:, :, 0], cact[:, :], ACT.Copy).then_inc(cact_hi, 1)
            split_to(2)
            act.wait_ge(loaded["router"], 16)
            fn(rh[:, :, :], router[:, :, :], ACT.Copy).then_inc(router_hi, 1)
            for l in range(2):
                o = result(act, ("pinT", l))
                read_out(fn(pinT[:, l], o[:, :].rearrange("p (k t) -> p k t", t=S), ACT.Copy), ("pinT", l))
            moved(act, "mod", 0)
            keep_ahead(act, ("mod", 1))
            act.wait_ge(*acol_ready.after(0))
            norm_out(0)

            qk_stats(0)
            for tt in range(TT):
                copy_out(("v", 0, tt), v[:, tt, :])
            for tt in range(TT):
                copy_out(("p", 0, tt), pin[:, tt, :])
            o = result(act, ("poolT",))
            read_out(fn(poolT, o[:, :].rearrange("p (c t) -> p c t", c=4), ACT.Copy), ("poolT",))
            for j in range(PAIRS):
                keep_ahead(act, ("score", 0, j))
                act.wait_ge(*nmax_ready.after(j))
                for e in range(2):
                    for part, (lo, hi) in enumerate(((0, S), (S, TRI))):
                        at = 128 + 16 * (j % 2) + 2 * part + e
                        last = fn(pr[:, j % 2, e, lo:hi], sc[:, j % 2, e, lo:hi], ACT.Exp, bias=stat[:, at:at + 1],
                                  accum_out=stat[:, at + 4:at + 5])
                last.then_inc(*exp_ready.mark(j))
                gate = gate_a if j < 2 else xn
                for tt in range(TT):
                    copy_out(("gate", j, tt), gate[:, tt, (j % 2) * 512:(j % 2 + 1) * 512])
                o = result(act, ("probT", j))
                read_out(fn(pT[:, j % 2], o[:, :].rearrange("p (e n) -> p e n", e=2)[:, :, 0:TRI], ACT.Copy), ("probT", j))
            for n in range(2):
                moved(act, "gate", 2 * n + 1, 0)
                moved(act, "gate", 2 * n + 1, 1)
                gate = (gate_a, xn)[n]
                fn(gate[:, :, :], gate[:, :, :], ACT.Sigmoid).then_inc(*sig_ready.mark(n))
            for n in range(2):
                copy_out(("grow", 0, n), gate_row[:, n * 512:(n + 1) * 512])
            for q in range(4):
                turned(("merged", 0, q // 2), ah[:, 2 * q:2 * q + 2, :], q)
            rms_std(1)
            for n in range(2):
                copy_out(("grow", 1, n), gate_row[:, n * 512:(n + 1) * 512])
            act.wait_ge(*acol_ready.after(1))
            norm_out(1)
            for j in range(FB0 // 2):
                if j >= 2:
                    act.wait_ge(*gT_ready.after(j - 2))
                for half in range(2):
                    for b in range(2):
                        blk = half * FB0 + 2 * j + b
                        o = result(act, ("up", j, half, b))
                        fn(cv[:, 2 * (j % 2) + half, b, :], o[:, 0:S], ACT.Identity, bias=col("conv_b", blk),
                           scale=col("conv_w", 2 * 2 * FB0 + blk)).then_inc(*taps_ready.mark(j, half, b))
                moved(act, "up", j, 0, 0)
                moved(act, "up", j, 0, 1)
                g = cv[:, 2 * (j % 2), :, :]
                fn(g, g, ACT.Silu).then_inc(*cg_ready.mark(j))
                act.wait_ge(*g_prod.after(j))
                fn(gh[:, 2 * j:2 * j + 2, :], prod, ACT.Copy).then_inc(*turn_his.mark("g", 0, j))

            for l in (1, 2):
                m0 = 2 + 3 * (l - 1)
                rms_std(m0)
                norm_out(m0)
                qk_stats(l)
                for tt in range(TT):
                    copy_out(("v", l, tt), v[:, tt, :])

                def u_out(n):
                    copy_out(("ucb", l, n), uF[:, n, :], S)

                def log_part(j):
                    moved(act, "score", l, j)
                    z, t = sc[:, j % 2], pr[:, j % 2]
                    then(fn(t, z, ACT.Abs))
                    then(fn(t, t, ACT.Exp, scale=-1.0))
                    fn(t, t, ACT.Ln, bias=1.0).then_inc(*ln_ready.mark(l, j))

                u_out(0)
                log_part(0)
                for n in (1, 2, 3):
                    u_out(n)
                for j in range(PAIRS):
                    moved(act, "later", l, j)
                    fn(pT[:, j % 2], sc[:, j % 2], ACT.Exp).then_inc(*weight_ready.mark(l, j))
                    if j < PAIRS - 1:
                        log_part(j + 1)
                def square(which, src, *keys):
                    for key in keys:
                        moved(act, key[0], l, *key[1:])
                    fn(sqF, src, ACT.Square).then_inc(*msq_ready.mark(l, which))

                def rms(which):
                    key = ("mean", l, which)
                    o = result(act, key)
                    if which == "attn":
                        act.wait_ge(*mixed_ready.after(l, "conv"))
                    read_out(fn(rsF, o[:, 0:S], ACT.Sqrt, bias=epsc[:, 0:1], scale=1.0 / AW), key)

                def high(which, src, at):
                    act.wait_ge(*scaled_ready.after(l, which))
                    fn(ah[:, at:at + 4, :], src, ACT.Copy).then_inc(*scaled_hi.mark(l, which))

                def pproj_out(n):
                    for tt in range(TT):
                        copy_out(("pproj", l, n, tt), pp[:, tt, n * 512:(n + 1) * 512])

                square("conv", convF, *(("ucb", n) for n in range(8, 12)))
                pproj_out(0)
                rms("conv")
                pproj_out(1)
                high("conv", convF, 4)
                square("attn", attnT, *(("attn", j) for j in range(PAIRS)))
                rms("attn")
                high("attn", attnT, 0)
                rms_std(m0 + 1)
                norm_out(m0 + 1)
                if l == 1:
                    def hidden_out(n):
                        o = result(act, ("gT", n))
                        for q in range(2):
                            fn(gh[:, 4 * n + 2 * q:4 * n + 2 * q + 2, :],
                               o[:, q * 512:(q + 1) * 512].rearrange("p (c t) -> p c t", t=S), ACT.Copy)\
                                .then_inc(*turn_his.mark("gT", n, q))

                    for n in range(NF):
                        for tt in range(TT):
                            copy_out(("d1", n, tt), g_tmp[:, 2 * (n % 2) + tt, :], func=ACT.Silu)
                        if n:
                            hidden_out(n - 1)
                    hidden_out(NF - 1)
                    rms_std(m0 + 2)
                    norm_out(m0 + 2)
                    for n in range(2):
                        for tt in range(TT):
                            copy_out(("pgate", l, n, tt), psig[:, 2 * tt + n, :], func=ACT.Sigmoid)

            keep_ahead(act, ("logits",))
            act.wait_ge(margin_ready, 1)
            fn(stat[:, 172:174], stat[:, 170:172], ACT.Exp).then_inc(margin_exp, 1)

            def expert_split(it, pos):
                n, s = NU + pos, NS + pos
                act.wait_ge(raw_loaded[n % RAW], it * (16 * 2 * UE // RAW) + 16 * (n // RAW + 1))
                act.wait_ge(unit_used, it * (2 * UE) + (s - HALF + 1))
                fn(whi[:, s % HALF, :], raw[:, n % RAW, :], ACT.Copy).then_inc(hi_ready, 1)

            def gathered_hi(i):
                act.wait_ge(e_xg, i + 1)
                fn(xh, xg, ACT.Copy).then_inc(e_xgh, 1)

            def expert(it, odd):
                i = it * 2 + odd
                done = [2]

                def e_result(name, n, c):
                    for pos in range(done[0], c + 2):
                        expert_split(it, odd * UE + pos)
                    done[0] = max(done[0], c + 2)
                    b, count = e_count(i, name, n)
                    act.wait_ge(e_filled[b], count)
                    return bank[b], e_drained[b]

                def turned_h(n, c):
                    o, _ = e_result("turn", n, c)
                    fn(eh[:, 4 * n:4 * n + 4, :], o[:, 0:512].rearrange("p (c t) -> p c t", c=4), ACT.Copy).then_inc(e_hi, 1)

                for n in range(NF):
                    o, free = e_result("gate", n, 4 * n + 2)
                    fn(sA[:, n % 2, :], o[:, :], ACT.Silu).then_inc(free, 1)
                    if n:
                        turned_h(n - 1, 4 * n + 2)
                turned_h(NF - 1, 4 * NF + 2)
                e_result("gather", 0, 4 * NF + 6)
                gathered_hi(i + 1)
                for n in range(2):
                    o, free = e_result("y", n, UE)
                    fn(yg[:, n * 512:(n + 1) * 512], o[:, :], ACT.Copy).then_inc(free, 1)

            def passes(first):
                with act.Fori(first // 2, (first + EXPERTS) // 2) as it:
                    for odd in range(2):
                        expert(it, odd)
                for b in (2, 3):
                    act.wait_ge(e_drained[b], (first + EXPERTS) * E_USES[b] + 1)

            split_to(NS)
            for pos in range(2):
                n, s = NU + pos, NS + pos
                act.wait_ge(raw_loaded[n % RAW], 16 * (n // RAW + 1))
                act.wait_ge(unit_used, s - HALF + 1)
                fn(whi[:, s % HALF, :], raw[:, n % RAW, :], ACT.Copy).then_inc(hi_ready, 1)
            gathered_hi(0)
            passes(0)
            act.wait_ge(flag_ready, 1)
            over = act.value_load(flag[0:1, 0:1], min_val=0, max_val=1)
            with act.If(over == 1):
                passes(EXPERTS)
            act.sem_inc(last_yg, 1)

            def tail_split(t):
                act.wait_ge(tail_loaded[t], 16)
                if t >= HALF:
                    act.wait_ge(tail_used, t - HALF + 1)
                fn(whi[:, t % HALF, :], raw[:, t % RAW, :], ACT.Copy).then_inc(tail_hi, 1)

            tail_split(0)
            tail_split(1)
            rms_std(7)
            norm_out(7)
            tail_split(2)
            tail_split(3)
            for n in range(2):
                for tt in range(TT):
                    copy_out(("pgate", 2, n, tt), psig[:, 2 * tt + n, :], func=ACT.Sigmoid)

        @block.vector
        def _(dve):
            V = nc.vector
            steps = [0]

            def then(ins):
                ins.then_inc(dve_step, 1)
                steps[0] += 1
                dve.wait_ge(dve_step, steps[0])

            def normalise(m):
                for tt in range(TT):
                    dve.wait_ge(*std_ready.after(m, tt))
                    at = 4 * m + 2 * tt + 1
                    r = stat[:, 32 + 2 * m + tt:33 + 2 * m + tt]
                    then(V.reciprocal(r, stat[:, at:at + 1]))
                    V.tensor_scalar(xn[:, tt, :], h[:, tt, :], r, None, ALU.mult).then_inc(*xn_ready.mark(m, tt))

            def norm_out(m):
                for q in range(4):
                    if q % 2 == 0:
                        key = ("norm", m, q // 2)
                        o = result(dve, key)
                    dve.wait_ge(*turn_his.after("norm", m, q))
                    two = slice(2 * q, 2 * q + 2)
                    if m < 2:
                        then(V.tensor_copy(ah[:, two, :], modulated[:, two, :]))
                        last = V.tensor_tensor(al[:, two, :], modulated[:, two, :], ah[:, two, :].bitcast(F32), ALU.subtract)
                    else:
                        for c in (2 * q, 2 * q + 1):
                            src = o[:, (c % 4) * S:(c % 4 + 1) * S]
                            last = V.scalar_tensor_tensor(out=al[:, c, :], in0=src, scalar=gain_of(m, c),
                                                          in1=ah[:, c, :].bitcast(F32), op0=ALU.mult, op1=ALU.subtract)
                    if q % 2:
                        read_out(last, key)

            split = [0]

            def split_to(n):
                for s in range(split[0], n):
                    at = split_at[s]
                    dve.wait_ge(hi_ready, s + 1)
                    V.tensor_tensor(wlo[:, s % HALF, :], raw[:, at % RAW, :], whi[:, s % HALF, :].bitcast(F32),
                                    ALU.subtract).then_inc(lo_ready, 1)
                split[0] = max(split[0], n)

            ahead.append((dve, split_to))

            def turned(key, hi, lo, step):
                o = result(dve, key)
                dve.wait_ge(*turn_his.after(*key[:2], step))
                return V.tensor_tensor(lo, o[:, (step % 2) * 512:(step % 2 + 1) * 512].rearrange("p (c t) -> p c t", t=S),
                                       hi.bitcast(F32), ALU.subtract)

            def modulation_rows(pc):
                for n in range(2):
                    o = result(dve, ("modrow", pc, n))
                    read_out(V.tensor_copy(mod_row[:, n * 512:(n + 1) * 512], o[0:2, :]), ("modrow", pc, n))

            def modulation(pc):
                o = result(dve, ("mod", pc))
                read_out(V.tensor_tensor(modc[:, pc * KD:(pc + 1) * KD], o[:, 0:KD], cols("ada_b", pc * KD, KD), ALU.add),
                         ("mod", pc))
                if pc in (1, 4):
                    moved(dve, "mod", pc)
                    g = pc // 3
                    V.scalar_tensor_tensor(out=acol[:, g, :], in0=modc[:, pc * KD:(pc + 1) * KD], scalar=1.0,
                                           in1=cols(("norm1_g", "norm2_g")[g], 0, KD), op0=ALU.add,
                                           op1=ALU.mult).then_inc(*acol_ready.mark(g))

            def qk_norm(l):
                for w in range(2):
                    for tt in range(TT):
                        at = 64 + 16 * (2 * w + tt)
                        dve.wait_ge(*qk_sq.after(l, w, tt))
                        V.reduce_sum(stat[:, at:at + 8], sq[:, tt, :].rearrange("p (h d) -> p h d", d=DH),
                                     AX).then_inc(*qk_sumsq.mark(l, w, tt))
                        dve.wait_ge(*qk_std.after(l, w, tt))
                        r = stat[:, 136 + 24:136 + 32]
                        then(V.reciprocal(r, stat[:, at + 8:at + 16]))
                        key = ("qk"[w], l, tt)
                        o = result(dve, key)
                        read_out(V.tensor_tensor(qkn[:, w, tt, :].rearrange("p (h d) -> p h d", d=DH),
                                                 o[:, :].rearrange("p (h d) -> p h d", d=DH),
                                                 r[:, :, None].broadcast_to([P, HEADS, DH]), ALU.mult), key)
                for w in range(2):
                    key = ("qkT", l, w)
                    o = result(dve, key)
                    read_out(V.tensor_scalar(qkT[:, w], o[:, :].rearrange("p (j t) -> p j t", t=S), col("qk_g", 2 * l + w),
                                             DH ** -0.5 if w == 0 else 1.0, ALU.mult, ALU.mult), key)

            def attn_out(l, j):
                key = ("attn", l, j)
                o = result(dve, key)
                read_out(V.tensor_copy(attnT[:, j, :], o[:, 0:S]), key)

            def pair(x, lo=0, hi=TRI):
                return x[:, :].rearrange("p (e n) -> p e n", e=2)[:, :, lo:hi]

            V.memset(epsc[:, :], EPS).then_inc(small_set, 1)
            V.memset(ones[:, :], 1.0).then_inc(small_set, 1)
            V.memset(relw[BUCKETS:BUCKETS + 1, :], 1.0).then_inc(small_set, 1)
            normalise(0)
            o = result(dve, ("vec",))
            read_out(V.tensor_copy(vec[:, :], o[:, 0:NVT * P]), ("vec",))
            o = result(dve, ("relv",))
            read_out(V.tensor_copy(relv[0:HEADS], o[0:HEADS, :]), ("relv",))
            dve.wait_ge(cact_hi, 1)
            V.tensor_tensor(cparts[:, :, 1], cact[:, :], cparts[:, :, 0].bitcast(F32), ALU.subtract).then_inc(cact_lo, 1)
            split_to(2)
            moved(dve, "vec")
            dve.wait_ge(router_hi, 1)
            V.tensor_tensor(rl[:, :, :], router[:, :, :], rh[:, :, :].bitcast(F32), ALU.subtract).then_inc(router_lo, 1)
            modulation_rows(0)
            modulation(0)
            modulation_rows(1)
            modulation(1)
            moved(dve, "mod", 0)
            dve.wait_ge(*acol_ready.after(0))
            norm_out(0)
            for n in range(4):
                o = result(dve, ("bias", n))
                s = o[:, :].rearrange("p (e k) -> p e k", e=2)
                V.tensor_copy(biasT[:, 2 * n:2 * n + 2, 0:S], s)
                read_out(V.tensor_copy(biasT[:, 2 * n:2 * n + 2, S:TRI], s[:, :, P:S]), ("bias", n))

            qk_norm(0)
            for n in range(4):
                moved(dve, "bias", n)

            def biased_scores(j):
                o = result(dve, ("score", 0, j))
                s = sc[:, j % 2]
                read_out(V.tensor_tensor(s, pair(o), biasT[:, 2 * j:2 * j + 2, :], ALU.add), ("score", 0, j))
                moved(dve, "score", 0, j)
                at = 128 + 16 * (j % 2)
                V.reduce_max(stat[:, at + 8:at + 10], s[:, :, 0:S], AX)
                then(V.reduce_max(stat[:, at + 10:at + 12], s[:, :, S:TRI], AX))
                V.tensor_scalar(stat[:, at:at + 4], stat[:, at + 8:at + 12], -1.0, None, ALU.mult)\
                    .then_inc(*nmax_ready.mark(j))

            def probabilities(j):
                dve.wait_ge(*exp_ready.after(j))
                at = 128 + 16 * (j % 2)
                then(V.reciprocal(stat[:, at + 12:at + 16], stat[:, at + 4:at + 8]))
                p = pr[:, j % 2]
                V.tensor_tensor(p[:, :, 0:S], p[:, :, 0:S], stat[:, at + 12:at + 14, None].broadcast_to([P, 2, S]), ALU.mult)
                V.tensor_tensor(p[:, :, S:TRI], p[:, :, S:TRI], stat[:, at + 14:at + 16, None].broadcast_to([P, 2, P]),
                                ALU.mult).then_inc(*prob_ready.mark(j))

            biased_scores(0)
            for g in range(2):
                key = ("poolF", g)
                o = result(dve, key)
                read_out(V.tensor_tensor(poolF[:, 2 * g:2 * g + 2, :], o[:, :].rearrange("p (g t) -> p g t", g=2),
                                         cols("pool_scale", 2 * g, 2)[:, :, None].broadcast_to([P, 2, S]), ALU.mult), key)
            for j in range(PAIRS):
                probabilities(j)
                modulation_rows(2 + j)
                if j < PAIRS - 1:
                    biased_scores(j + 1)
                modulation(2 + j)
                attn_out(0, j)
            for n in range(2):
                dve.wait_ge(*sig_ready.after(n))
            for n in range(2):
                for tt in range(TT):
                    ga, gp = (g[:, tt, n * 512:(n + 1) * 512] for g in (gate_a, xn))
                    for nm, g in (("ba", ga), ("bp", gp)):
                        o = result(dve, (nm, n, tt))
                        read_out(V.tensor_tensor(g, g, o[:, :], ALU.mult), (nm, n, tt))
                    moved(dve, "ba", n, tt)
                    moved(dve, "bp", n, tt)
                    V.tensor_tensor(ga, ga, gp, ALU.add).then_inc(*merged_ready.mark(n, tt))
            for q in range(4):
                last = turned(("merged", 0, q // 2), ah[:, 2 * q:2 * q + 2, :], al[:, 2 * q:2 * q + 2, :], q)
                if q % 2:
                    read_out(last, ("merged", 0, q // 2))

            def gated_rows(name, m, order, tmp):
                for k, (n, tt) in enumerate(order):
                    key = (name, 0, n, tt)
                    o = result(dve, key)
                    t = tmp[:, k % 2, :]
                    hh = h[:, tt, n * 512:(n + 1) * 512]
                    read_out(V.tensor_tensor(t, o[:, :], gate_row[:, n * 512:(n + 1) * 512], ALU.mult), key)
                    moved(dve, *key)
                    last = V.tensor_tensor(hh, hh, t, ALU.add)
                    if n == 0:
                        then(last)
                    else:
                        last.then_inc(*h_ready.mark(m, tt))

            BY_N = [(n, tt) for n in range(2) for tt in range(TT)]
            BY_T = [(n, tt) for tt in range(TT) for n in range(2)]
            for n in range(2):
                moved(dve, "grow", 0, n)
            gated_rows("out", 1, BY_N, sq)
            normalise(1)
            dve.wait_ge(*acol_ready.after(1))
            norm_out(1)
            for j in range(FB0 // 2):
                for half in range(2):
                    for b in range(2):
                        blk = half * FB0 + 2 * j + b
                        key = ("up", j, half, b)
                        o = result(dve, key)
                        dve.wait_ge(*taps_ready.after(j, half, b))
                        y = cv[:, 2 * (j % 2) + half, b, :]
                        then(V.scalar_tensor_tensor(out=y[:, 1:S], in0=o[:, 0:S - 1], scalar=col("conv_w", 2 * FB0 + blk),
                                                    in1=y[:, 1:S], op0=ALU.mult, op1=ALU.add))
                        read_out(V.scalar_tensor_tensor(out=y[:, 2:S], in0=o[:, 0:S - 2], scalar=col("conv_w", blk),
                                                        in1=y[:, 2:S], op0=ALU.mult, op1=ALU.add), key)
                dve.wait_ge(*cg_ready.after(j))
                moved(dve, "up", j, 1, 0)
                moved(dve, "up", j, 1, 1)
                V.tensor_tensor(prod, cv[:, 2 * (j % 2)], cv[:, 2 * (j % 2) + 1], ALU.mult).then_inc(*g_prod.mark(j))
                dve.wait_ge(*turn_his.after("g", 0, j))
                V.tensor_tensor(gl[:, 2 * j:2 * j + 2, :], prod, gh[:, 2 * j:2 * j + 2, :].bitcast(F32), ALU.subtract)\
                    .then_inc(*gT_ready.mark(j))
            for n in range(2):
                moved(dve, "grow", 1, n)
            gated_rows("down", 2, BY_T, g_tmp)

            def add_rows(name, l, order):
                for n, tt in order:
                    key = (name, l, n, tt)
                    o = result(dve, key)
                    hh = h[:, tt, n * 512:(n + 1) * 512]
                    read_out(V.tensor_tensor(hh, hh, o[:, :], ALU.add), key)

            def gate_ple(l, m):
                for n, tt in BY_N:
                    key = ("pgate", l, n, tt)
                    moved(dve, *key)
                    t = psig[:, 2 * tt + n, :]
                    hh = h[:, tt, n * 512:(n + 1) * 512]
                    then(V.tensor_tensor(t, t, pp[:, tt, n * 512:(n + 1) * 512], ALU.mult))
                    last = V.tensor_tensor(hh, hh, t, ALU.add)
                    if n == 0:
                        then(last)
                    else:
                        last.then_inc(*h_ready.mark(m, tt))

            for l in (1, 2):
                li = l - 1
                m0 = 2 + 3 * li
                normalise(m0)
                norm_out(m0)
                qk_norm(l)

                def masked_scores(j):
                    key = ("score", l, j)
                    o = result(dve, key)
                    read_out(V.tensor_tensor(sc[:, j % 2], pair(o), mask[:, None, :].broadcast_to([P, 2, TRI]), ALU.add), key)

                def softplus(j):
                    dve.wait_ge(*ln_ready.after(l, j))
                    V.scalar_tensor_tensor(out=pr[:, j % 2], in0=sc[:, j % 2], scalar=0.0, in1=pr[:, j % 2],
                                           op0=ALU.max, op1=ALU.add).then_inc(*sp_ready.mark(l, j))

                def ucb(n):
                    b = n % 4
                    key = ("ucb", l, n)
                    if n < 8:
                        moved(dve, "ucb", l, b)
                        o = result(dve, key)
                        read_out(V.tensor_tensor(cuF[:, b, :], o[:, 0:S], uF[:, b, :], ALU.mult), key)
                        moved(dve, *key)
                        y, x = convF[:, b, :], cuF[:, b, :]
                        tap = [col("conv_w2", 12 * li + 4 * t + b) for t in range(3)]
                        then(V.tensor_scalar(y, x, tap[2], col("conv_b2", 4 * li + b), ALU.mult, ALU.add))
                        then(V.scalar_tensor_tensor(out=y[:, 1:S], in0=x[:, 0:S - 1], scalar=tap[1], in1=y[:, 1:S],
                                                    op0=ALU.mult, op1=ALU.add))
                        then(V.scalar_tensor_tensor(out=y[:, 2:S], in0=x[:, 0:S - 2], scalar=tap[0], in1=y[:, 2:S],
                                                    op0=ALU.mult, op1=ALU.add))
                    else:
                        o = result(dve, key)
                        read_out(V.tensor_tensor(convF[:, b, :], convF[:, b, :], o[:, 0:S], ALU.mult), key)

                masked_scores(0)
                softplus(0)
                for j in range(PAIRS):
                    key = ("later", l, j)
                    o = result(dve, key)
                    read_out(V.tensor_tensor(sc[:, j % 2], sc[:, j % 2], pair(o), ALU.subtract), key)
                    if j < PAIRS - 1:
                        masked_scores(j + 1)
                        softplus(j + 1)
                        for n in ((4, 5, 6), (7, 8, 9), (10, 11))[j]:
                            ucb(n)
                        attn_out(l, j)
                for which, src, at, gname in (("conv", convF, 4, "conv_g"), ("attn", attnT, 0, "attn_g")):
                    if which == "attn":
                        attn_out(l, PAIRS - 1)
                    moved(dve, "mean", l, which)
                    then(V.reciprocal(rsF, rsF))
                    for c in range(CA):
                        last = V.scalar_tensor_tensor(out=src[:, c, :], in0=src[:, c, :], scalar=col(gname, 4 * li + c),
                                                      in1=rsF, op0=ALU.mult, op1=ALU.mult)
                    last.then_inc(*scaled_ready.mark(l, which))
                    dve.wait_ge(*scaled_hi.after(l, which))
                    V.tensor_tensor(al[:, at:at + 4, :], src, ah[:, at:at + 4, :].bitcast(F32), ALU.subtract)\
                        .then_inc(*mixed_ready.mark(l, which))
                add_rows("wo", l, BY_N)
                normalise(m0 + 1)
                norm_out(m0 + 1)
                if l == 1:
                    def hidden_out(n):
                        for q in range(2):
                            at = 4 * n + 2 * q
                            last = turned(("gT", n), gh[:, at:at + 2, :], gl[:, at:at + 2, :], q)
                        read_out(last, ("gT", n))

                    for n in range(NF):
                        if n:
                            hidden_out(n - 1)
                        for tt in range(TT):
                            moved(dve, "d1", n, tt)
                            key = ("d3", n, tt)
                            o = result(dve, key)
                            read_out(V.tensor_tensor(g_mul[:, tt, :], g_tmp[:, 2 * (n % 2) + tt, :], o[:, :], ALU.mult), key)
                    hidden_out(NF - 1)
                    add_rows("d2", 0, BY_T)
                    normalise(m0 + 2)
                    norm_out(m0 + 2)
                    gate_ple(1, 5)

            LG, LG2, EQ, ONE1, ONE2, SH, CHO, T = (choice[:, k] for k in range(8))
            rankb = rank[:, None, :].broadcast_to([P, TT, EXPERTS])

            def spread(x):
                return x[:, :, None].broadcast_to([P, TT, EXPERTS])

            o = result(dve, ("logits",))
            read_out(V.tensor_copy(LG, o[:, 0:16].rearrange("p (t e) -> p t e", t=TT)), ("logits",))
            moved(dve, "logits")
            for lg, one, top in ((LG, ONE1, stat[:, 180:182]), (LG2, ONE2, stat[:, 182:184])):
                then(V.reduce_max(top, lg, AX))
                then(V.tensor_tensor(EQ, lg, spread(top), ALU.is_equal))
                then(V.tensor_tensor(EQ, EQ, rankb, ALU.mult))
                then(V.reduce_max(stat[:, 184:186], EQ, AX))
                then(V.tensor_tensor(one, spread(stat[:, 184:186]), rankb, ALU.is_equal))
                if lg is LG:
                    then(V.scalar_tensor_tensor(out=LG2, in0=one, scalar=FAR, in1=LG, op0=ALU.mult, op1=ALU.add))
            V.tensor_tensor(stat[:, 170:172], stat[:, 182:184], stat[:, 180:182], ALU.subtract).then_inc(margin_ready, 1)
            V.tensor_tensor(CHO, ONE1, ONE2, ALU.add).then_inc(chosen_ready, 1)
            dve.wait_ge(margin_exp, 1)
            then(V.tensor_scalar(stat[:, 174:176], stat[:, 172:174], 1.0, None, ALU.add))
            then(V.reciprocal(stat[:, 176:178], stat[:, 174:176]))
            then(V.tensor_tensor(stat[:, 178:180], stat[:, 172:174], stat[:, 176:178], ALU.mult))
            then(V.tensor_tensor(ONE1, ONE1, spread(stat[:, 176:178]), ALU.mult))
            then(V.tensor_tensor(ONE2, ONE2, spread(stat[:, 178:180]), ALU.mult))
            then(V.memset(share_of[:, :, :], 0.0))
            V.tensor_tensor(share_of[:, :, 0:8], ONE1, ONE2, ALU.add)
            then(V.tensor_tensor(share_of[:, :, 8:16], ONE1, ONE2, ALU.add))
            then(V.memset(slot_of[:, :, :], -1.0))
            o = result(dve, ("slots",))
            then(V.scalar_tensor_tensor(out=T, in0=o[:, 0:16].rearrange("p (t e) -> p t e", t=TT), scalar=1.0, in1=CHO,
                                        op0=ALU.add, op1=ALU.mult))
            V.tensor_scalar(slot_of[:, :, 0:8], T, -1.0, None, ALU.add)
            then(V.tensor_scalar(slot_of[:, :, 8:16], T, -1.0 - P, None, ALU.add))
            then(V.reduce_max(stat[:, 190:191], o[:, 16:24], AX))
            read_out(V.tensor_scalar(flag[:, 0:1], stat[:, 190:191], float(P), None, ALU.is_gt), ("slots",))
            moved(dve, "slots")
            dve.sem_inc(flag_ready, 1)

            def pick_tokens(i):
                for tt in range(TT):
                    V.tensor_scalar(pshare[:, tt, :], iota, slot_of[:, tt, bass.ds(i, 1)], share_of[:, tt, bass.ds(i, 1)],
                                    ALU.is_equal, ALU.mult)
                for tt in range(TT):
                    last = V.tensor_scalar(pick[:, tt, :], iota, slot_of[:, tt, bass.ds(i, 1)], None, ALU.is_equal)
                last.then_inc(e_pick, 1)

            def gathered(i):
                V.tensor_tensor(xg, wide[0][:, :].rearrange("p (c t) -> p c t", t=P),
                                cols("ffn_g", KD, KD)[:, :, None].broadcast_to([P, KD, P]), ALU.mult).then_inc(e_xg, 1)
                dve.wait_ge(e_xgh, i + 1)
                V.tensor_tensor(xl, xg, xh.bitcast(F32), ALU.subtract).then_inc(e_xgl, 1)

            def expert_split(it, pos):
                s = NS + pos
                dve.wait_ge(hi_ready, it * (2 * UE) + (s + 1))
                V.tensor_tensor(wlo[:, s % HALF, :], raw[:, (NU + pos) % RAW, :], whi[:, s % HALF, :].bitcast(F32),
                                ALU.subtract).then_inc(lo_ready, 1)

            def expert_split_first(pos):
                s = NS + pos
                dve.wait_ge(hi_ready, s + 1)
                V.tensor_tensor(wlo[:, s % HALF, :], raw[:, (NU + pos) % RAW, :], whi[:, s % HALF, :].bitcast(F32),
                                ALU.subtract).then_inc(lo_ready, 1)

            split_to(NS)
            for pos in range(2):
                expert_split_first(pos)
            V.memset(yg, 0.0).then_inc(e_zeroed, 1)
            V.memset(shareT, 0.0).then_inc(e_zeroed, 1)
            pick_tokens(0)
            dve.wait_ge(e_filled[X], 1)
            gathered(0)
            dve.sem_inc(e_drained[X], 1)

            def expert(it, odd):
                i = it * 2 + odd
                done = [2]

                def keep_up(c):
                    for pos in range(done[0], c + 2):
                        expert_split(it, odd * UE + pos)
                    done[0] = max(done[0], c + 2)

                def e_result(name, n, c):
                    keep_up(c)
                    b, count = e_count(i, name, n)
                    dve.wait_ge(e_filled[b], count)
                    return bank[b], e_drained[b]

                def turned_h(n, c):
                    o, free = e_result("turn", n, c)
                    dve.wait_ge(e_hi, i * NF + (n + 1))
                    V.tensor_tensor(el[:, 4 * n:4 * n + 4, :], o[:, 0:512].rearrange("p (c t) -> p c t", c=4),
                                    eh[:, 4 * n:4 * n + 4, :].bitcast(F32), ALU.subtract).then_inc(free, 1)

                for tt in range(TT):
                    o, free = e_result("rows", tt, 2)
                    V.tensor_tensor(h[:, tt, :], h[:, tt, :], o[:, :], ALU.add).then_inc(free, 1)
                o, free = e_result("share", 0, 2)
                V.tensor_copy(shareT, o[:, 0:S].rearrange("p (t s) -> p t s", t=TT)).then_inc(free, 1)
                pick_tokens(i + 1)
                for n in range(NF):
                    if n:
                        turned_h(n - 1, 4 * n + 2)
                    keep_up(4 * n + 4)
                    b, count = e_count(i, "gate", n)
                    dve.wait_ge(e_drained[b], count)
                    o, free = e_result("up", n, 4 * n + 4)
                    V.tensor_tensor(hm[:, n % 2, :], sA[:, n % 2, :], o[:, :], ALU.mult).then_inc(free, 1)
                turned_h(NF - 1, 4 * NF + 2)
                o, free = e_result("gather", 0, 4 * NF + 6)
                gathered(i + 1)
                dve.sem_inc(free, 1)
                keep_up(UE)

            def passes(first):
                with dve.Fori(first // 2, (first + EXPERTS) // 2) as it:
                    for odd in range(2):
                        expert(it, odd)
                dve.wait_ge(e_drained[X], (first + EXPERTS) * E_USES[X] + 1)
                dve.wait_ge(e_drained[Y], (first + EXPERTS) * E_USES[Y] + 1)

            passes(0)
            over = dve.value_load(flag[0:1, 0:1], min_val=0, max_val=1)
            with dve.If(over == 1):
                passes(EXPERTS)
            dve.sem_inc(last_share, 1)
            for tt in range(TT):
                dve.wait_ge(last_rows, tt + 1)
                V.tensor_tensor(h[:, tt, :], h[:, tt, :], wide[tt][:, :], ALU.add).then_inc(*h_ready.mark(7, tt))

            def tail_split(t):
                dve.wait_ge(tail_hi, t + 1)
                V.tensor_tensor(wlo[:, t % HALF, :], raw[:, t % RAW, :], whi[:, t % HALF, :].bitcast(F32),
                                ALU.subtract).then_inc(tail_lo, 1)

            tail_split(0)
            tail_split(1)
            normalise(7)
            norm_out(7)
            tail_split(2)
            tail_split(3)
            gate_ple(2, 8)


_NAMES = ['x', 'ada_w', 'w_in', 'rel_bias', 'pool_w', 'w_branch_attn', 'w_branch_pool', 'w_out', 'w_up', 'w_down',
          'p_2', 'w_in_2', 'w_o_2', 'dense_w1_2', 'dense_w3_2', 'dense_w2_2', 'router_w_2', 'moe_w1_2', 'moe_w3_2',
          'moe_w2_2', 'ple_gate_w_2', 'ple_proj_w_2', 'vector_rows', 'shape_consts', 'shape_buckets']


def kernel(**inputs):
    import concourse.bacc as _bacc
    from concourse.bass_utils import run_bass_kernel_spmd as _run

    given = {k: np.ascontiguousarray(v) for k, v in inputs.items()}
    gains = [np.tile(given[n][l], 2) for n, l in (("q_norm_g", 0), ("k_norm_g", 0), ("q_norm_g_2", 0),
                                                 ("k_norm_g_2", 0), ("q_norm_g_2", 1), ("k_norm_g_2", 1))]
    rows = {"ada_b": given["ada_b"], "norm1_g": given["norm1_g"], "norm2_g": given["norm2_g"], "c": given["c"],
            "pool_scale": given["pool_scale"], "conv_w": given["conv_w"], "conv_b": given["conv_b"],
            "mix_g": given["mix_norm_g_2"], "ffn_g": given["ffn_norm_g_2"], "ple_g": given["ple_norm_g_2"],
            "attn_g": given["attn_out_g_2"], "conv_g": given["conv_out_g_2"], "conv_w2": given["conv_w_2"],
            "conv_b2": given["conv_b_2"], "qk_g": np.stack(gains)}
    rows = [rows[n].reshape(-1, P) for n in VROWS]
    rows.append(np.zeros((NVT * P - sum(len(r) for r in rows), P), np.float32))
    given["vector_rows"] = np.concatenate(rows)
    given["shape_consts"], given["shape_buckets"] = shape_constants()

    nc = _bacc.Bacc("TRN2", target_bir_lowering=False, num_devices=1)
    arrays, args = {}, {}
    for name in _NAMES:
        v = given[name]
        arrays[f"in_{name}"] = v
        args[name] = nc.dram_tensor(f"in_{name}", v.shape, mybir.dt.from_np(v.dtype), kind="ExternalInput").ap()
    out = nc.dram_tensor("out", (1, S, D), F32, kind="ExternalOutput").ap()
    fused_blocks(nc, args, out)
    r = _run(nc, [arrays], core_ids=[0])
    return r.results[0]["out"]
```
